# Optimizing a Trainium2 kernel written in Bass

```python
import jax, jax.numpy as jnp
from jax import lax
import numpy as np

D_MODEL = 1024
BATCH = 1
SEQ = 256
DEPTH = 2
DEC_BATCH = 8
DEC_SEQ = 8
PAST_LEN = 2048
PAGE_SIZE = 128

N_MIXERS = 2
N_LAYERS_A = (DEPTH + 1) // 2
N_LAYERS_B = DEPTH // 2
A_HEADS = 8
A_KEY = 128
A_VAL = D_MODEL // A_HEADS
B_HEADS = 4
B_KEY = D_MODEL // 2 // B_HEADS
B_VAL = D_MODEL // B_HEADS
B_GATE_RANK = 16
B_GATE_NORMALIZER = 16.0
CHUNK = 16
MEM_LEN = 256
X_HEADS = 4
X_HEAD_DIM = D_MODEL // X_HEADS
N_EXPERTS = 16
N_GROUPS = 4
EXPERTS_PER_GROUP = N_EXPERTS // N_GROUPS
TOP_K = 2
D_EXPERT = 512
DN_ALPHA = (2 * DEPTH) ** 0.25
DN_BETA = (8 * DEPTH) ** -0.25
LN_EPS = 1e-5
RMS_EPS = 1e-6

A_IN = 2 * A_HEADS * A_KEY + A_HEADS * A_VAL + D_MODEL
B_IN = 2 * B_HEADS * B_KEY + B_HEADS * B_VAL + D_MODEL + B_GATE_RANK

kernel_name = "hgrn2_gla_memxattn_grouped_moe_step"

F32 = jnp.float32

def chunked_gated_linear_attention(q, k, v, g, s0):
    B, T, H, K = q.shape
    V = v.shape[-1]
    c = min(CHUNK, T)
    n = -(-T // c)
    pad = n * c - T
    if pad:
        pw = ((0, 0), (0, pad), (0, 0), (0, 0))
        q, k, v, g = (jnp.pad(a, pw) for a in (q, k, v, g))
    qc = q.reshape(B, n, c, H, K).transpose(0, 1, 3, 2, 4)
    kc = k.reshape(B, n, c, H, K).transpose(0, 1, 3, 2, 4)
    gc = g.reshape(B, n, c, H, K).transpose(0, 1, 3, 2, 4)
    vc = v.reshape(B, n, c, H, V).transpose(0, 1, 3, 2, 4)
    b = jnp.cumsum(gc, axis=3)
    b_mid = b[:, :, :, c // 2:c // 2 + 1, :]
    scores = jnp.einsum('bnhik,bnhjk->bnhij', qc * jnp.exp(b - b_mid), kc * jnp.exp(b_mid - b))
    causal = jnp.tril(jnp.ones((c, c), dtype=bool))
    scores = jnp.where(causal, scores, 0.0)
    o_intra = jnp.einsum('bnhij,bnhjv->bnhiv', scores, vc)
    q_inter = qc * jnp.exp(b)
    b_last = b[:, :, :, -1, :]
    k_state = kc * jnp.exp(b_last[:, :, :, None, :] - b)

    def step(S, inp):
        q_i, k_i, v_i, bl = inp
        o = jnp.einsum('bhck,bhkv->bhcv', q_i, S)
        S = jnp.exp(bl)[..., None] * S + jnp.einsum('bhck,bhcv->bhkv', k_i, v_i)
        return S, o

    S, o_inter = lax.scan(step, s0,
                          (jnp.moveaxis(q_inter, 1, 0), jnp.moveaxis(k_state, 1, 0),
                           jnp.moveaxis(vc, 1, 0), jnp.moveaxis(b_last, 1, 0)))
    o = o_intra + jnp.moveaxis(o_inter, 0, 1)
    o = o.transpose(0, 1, 3, 2, 4).reshape(B, n * c, H, V)[:, :T]
    return o, S

def gated_rmsnorm(o, gate, gain):
    o = o * lax.rsqrt(jnp.mean(o * o, axis=-1, keepdims=True) + RMS_EPS)
    return o * gain.astype(F32) * jax.nn.silu(gate.astype(F32))

def hgrn2_mixer(x, s0, w_in, lb, norm_g, w_out):
    B, T, _ = x.shape
    hk = A_HEADS * A_KEY
    proj = x @ w_in
    q, f, i, gate = jnp.split(proj, [hk, 2 * hk, 2 * hk + A_HEADS * A_VAL], axis=-1)
    q = jax.nn.silu(q.astype(F32)).reshape(B, T, A_HEADS, A_KEY) * (A_KEY ** -0.5)
    fg = lb + (1.0 - lb) * jax.nn.sigmoid(f.astype(F32))
    k = (1.0 - fg).reshape(B, T, A_HEADS, A_KEY)
    logf = jnp.log(fg).reshape(B, T, A_HEADS, A_KEY)
    v = i.astype(F32).reshape(B, T, A_HEADS, A_VAL)
    o, s = chunked_gated_linear_attention(q, k, v, logf, s0.astype(F32))
    o = gated_rmsnorm(o, gate.reshape(B, T, A_HEADS, A_VAL), norm_g)
    return o.reshape(B, T, A_HEADS * A_VAL).astype(x.dtype) @ w_out, s.astype(s0.dtype)

def gla_mixer(x, s0, w_in, w_gk2, b_gk2, norm_g, w_out):
    B, T, _ = x.shape
    hk = B_HEADS * B_KEY
    hv = B_HEADS * B_VAL
    proj = x @ w_in
    q, k, v, gate, lr = jnp.split(proj, [hk, 2 * hk, 2 * hk + hv, 2 * hk + hv + D_MODEL], axis=-1)
    gk = jax.nn.log_sigmoid((lr @ w_gk2 + b_gk2).astype(F32)) / B_GATE_NORMALIZER
    q = q.astype(F32).reshape(B, T, B_HEADS, B_KEY) * (B_KEY ** -0.5)
    k = k.astype(F32).reshape(B, T, B_HEADS, B_KEY)
    v = v.astype(F32).reshape(B, T, B_HEADS, B_VAL)
    o, s = chunked_gated_linear_attention(q, k, v, gk.reshape(B, T, B_HEADS, B_KEY), s0.astype(F32))
    o = gated_rmsnorm(o, gate.reshape(B, T, B_HEADS, B_VAL), norm_g)
    return o.reshape(B, T, hv).astype(x.dtype) @ w_out, s.astype(s0.dtype)

def memory_kv(mem, w_kv):
    B, M, _ = mem.shape
    kv = (mem @ w_kv).reshape(B, M, 2, X_HEADS, X_HEAD_DIM)
    return kv[:, :, 0], kv[:, :, 1]

def memory_cross_attention(x, mem_k, mem_v, w_q, w_o):
    B, T, _ = x.shape
    q = (x @ w_q).reshape(B, T, X_HEADS, X_HEAD_DIM)
    s = jnp.einsum('bthd,bmhd->bhtm', q, mem_k).astype(F32) * (X_HEAD_DIM ** -0.5)
    p = jax.nn.softmax(s, axis=-1).astype(x.dtype)
    o = jnp.einsum('bhtm,bmhd->bthd', p, mem_v).reshape(B, T, D_MODEL)
    return o @ w_o

def grouped_moe(x, router_w, router_bias, w_gate, w_up, w_down):
    scores = jax.nn.sigmoid((x @ router_w).astype(F32))
    sel = scores + router_bias.astype(F32)
    grouped = sel.reshape(*sel.shape[:-1], N_GROUPS, EXPERTS_PER_GROUP)
    group_score = lax.top_k(grouped, TOP_K)[0].sum(-1)
    best = jnp.argmax(group_score, axis=-1)
    in_group = (jnp.arange(N_EXPERTS) // EXPERTS_PER_GROUP) == best[..., None]
    _, idx = lax.top_k(jnp.where(in_group, sel, -jnp.inf), TOP_K)
    w = jnp.take_along_axis(scores, idx, axis=-1)
    w = w / jnp.sum(w, axis=-1, keepdims=True)
    combine = jnp.sum(jax.nn.one_hot(idx, N_EXPERTS, dtype=F32) * w[..., None], axis=-2)
    y = jnp.zeros(x.shape, F32)
    for e in range(N_EXPERTS):
        h = jax.nn.silu(x @ w_gate[e]) * (x @ w_up[e])
        y = y + combine[..., e:e + 1] * (h @ w_down[e]).astype(F32)
    return y.astype(x.dtype)

def post_norm(x, h, g, b):
    z = (DN_ALPHA * x + h).astype(F32)
    mu = jnp.mean(z, axis=-1, keepdims=True)
    var = jnp.mean(jnp.square(z - mu), axis=-1, keepdims=True)
    z = (z - mu) * lax.rsqrt(var + LN_EPS)
    return (z * g.astype(F32) + b.astype(F32)).astype(x.dtype)

def setup_inputs(seed: int = 0) -> dict:
    key = jax.random.key(seed)
    ks = iter(jax.random.split(key, 32))

    def nrm(shape, scale):
        return jax.random.normal(next(ks), shape, F32) * scale

    D = D_MODEL
    return {
        "x_prompt": nrm((BATCH, SEQ, D), 1.0),
        "x_sample": nrm((DEC_BATCH, DEC_SEQ, D), 1.0),
        "state_hgrn": nrm((N_LAYERS_A, DEC_BATCH, A_HEADS, A_KEY, A_VAL), 0.5),
        "state_gla": nrm((N_LAYERS_B, DEC_BATCH, B_HEADS, B_KEY, B_VAL), 1.0),
        "cache_mem_k": nrm((DEPTH, DEC_BATCH, MEM_LEN, X_HEADS, X_HEAD_DIM), 1.0),
        "cache_mem_v": nrm((DEPTH, DEC_BATCH, MEM_LEN, X_HEADS, X_HEAD_DIM), 1.0),
        "mem_prompt": nrm((BATCH, MEM_LEN, D), 1.0),
        "hgrn_w_in": nrm((N_LAYERS_A, D, A_IN), D ** -0.5),
        "hgrn_lb_logits": nrm((DEPTH + 1, A_HEADS * A_KEY), 0.1),
        "hgrn_norm_g": 1.0 + nrm((N_LAYERS_A, A_VAL), 0.02),
        "hgrn_w_out": nrm((N_LAYERS_A, A_HEADS * A_VAL, D), DN_BETA * (A_HEADS * A_VAL) ** -0.5),
        "gla_w_in": nrm((N_LAYERS_B, D, B_IN), D ** -0.5),
        "gla_w_gk2": nrm((N_LAYERS_B, B_GATE_RANK, B_HEADS * B_KEY), B_GATE_RANK ** -0.5),
        "gla_b_gk2": nrm((N_LAYERS_B, B_HEADS * B_KEY), 0.02),
        "gla_norm_g": 1.0 + nrm((N_LAYERS_B, B_VAL), 0.02),
        "gla_w_out": nrm((N_LAYERS_B, B_HEADS * B_VAL, D), DN_BETA * (B_HEADS * B_VAL) ** -0.5),
        "xattn_w_q": nrm((DEPTH, D, D), D ** -0.5),
        "xattn_w_kv": nrm((DEPTH, D, 2 * D), D ** -0.5),
        "xattn_w_o": nrm((DEPTH, D, D), DN_BETA * D ** -0.5),
        "router_w": nrm((D, N_EXPERTS), D ** -0.5),
        "router_bias": nrm((N_EXPERTS,), 0.01),
        "moe_w_gate": nrm((DEPTH, N_EXPERTS, D, D_EXPERT), D ** -0.5),
        "moe_w_up": nrm((DEPTH, N_EXPERTS, D, D_EXPERT), D ** -0.5),
        "moe_w_down": nrm((DEPTH, N_EXPERTS, D_EXPERT, D), DN_BETA * D_EXPERT ** -0.5),
        "ln_g": 1.0 + nrm((DEPTH, 3, D), 0.02),
        "ln_b": nrm((DEPTH, 3, D), 0.02),
    }

def reference(x_prompt, x_sample, state_hgrn, state_gla, cache_mem_k, cache_mem_v, mem_prompt,
              hgrn_w_in, hgrn_lb_logits, hgrn_norm_g, hgrn_w_out,
              gla_w_in, gla_w_gk2, gla_b_gk2, gla_norm_g, gla_w_out,
              xattn_w_q, xattn_w_kv, xattn_w_o,
              router_w, router_bias, moe_w_gate, moe_w_up, moe_w_down,
              ln_g, ln_b):
    lb_all = jnp.cumsum(jax.nn.softmax(hgrn_lb_logits.astype(F32), axis=0), axis=0)

    def run_trunk(x, states_a, states_b, mem_ks, mem_vs):
        new_a, new_b = [], []
        for l in range(DEPTH):
            j = l // N_MIXERS
            if l % N_MIXERS == 0:
                h, s = hgrn2_mixer(x, states_a[j], hgrn_w_in[j], lb_all[l], hgrn_norm_g[j], hgrn_w_out[j])
                new_a.append(s)
            else:
                h, s = gla_mixer(x, states_b[j], gla_w_in[j], gla_w_gk2[j], gla_b_gk2[j],
                                 gla_norm_g[j], gla_w_out[j])
                new_b.append(s)
            x = post_norm(x, h, ln_g[l, 0], ln_b[l, 0])
            c = memory_cross_attention(x, mem_ks[l], mem_vs[l], xattn_w_q[l], xattn_w_o[l])
            x = post_norm(x, c, ln_g[l, 1], ln_b[l, 1])
            m = grouped_moe(x, router_w, router_bias, moe_w_gate[l], moe_w_up[l], moe_w_down[l])
            x = post_norm(x, m, ln_g[l, 2], ln_b[l, 2])
        return x, jnp.stack(new_a), jnp.stack(new_b)

    pkv = [memory_kv(mem_prompt, xattn_w_kv[l]) for l in range(DEPTH)]
    mem_k_prompt = jnp.stack([kv[0] for kv in pkv])
    mem_v_prompt = jnp.stack([kv[1] for kv in pkv])
    za = jnp.zeros((N_LAYERS_A, BATCH, A_HEADS, A_KEY, A_VAL), x_prompt.dtype)
    zb = jnp.zeros((N_LAYERS_B, BATCH, B_HEADS, B_KEY, B_VAL), x_prompt.dtype)
    y_prompt, state_hgrn_prompt, state_gla_prompt = run_trunk(x_prompt, za, zb, mem_k_prompt, mem_v_prompt)

    y_sample, state_hgrn_sample, state_gla_sample = run_trunk(x_sample, state_hgrn, state_gla,
                                                              cache_mem_k, cache_mem_v)

    return (y_prompt, y_sample, state_hgrn_prompt, state_gla_prompt, mem_k_prompt, mem_v_prompt,
            state_hgrn_sample, state_gla_sample)


_drawn_inputs = setup_inputs


def setup_inputs(seed=0):
    import zlib

    import numpy as np

    out = dict(_drawn_inputs(seed))
    spreads = {}
    factors = {'hgrn_norm_g': 3.232, 'gla_b_gk2': 6.455, 'gla_norm_g': 8.0}
    for name, (base, spread) in spreads.items():
        noise = np.random.default_rng([zlib.crc32(name.encode()), seed]).standard_normal(out[name].shape)
        drawn = base * np.exp(spread * noise) if base else spread * noise
        out[name] = __import__('jax').numpy.asarray(drawn.astype(out[name].dtype))
    for name, factor in factors.items():
        out[name] = (out[name] * factor).astype(out[name].dtype)
    return out
```

```python
from contextlib import ExitStack

import concourse.bass as bass
from concourse import mybir

F32 = mybir.dt.float32
F32R = mybir.dt.float32r
I32 = mybir.dt.int32
U32 = mybir.dt.uint32
ACT = mybir.ActivationFunctionType
ALU = mybir.AluOpType
AX_X = mybir.AxisListType.X

P = 128
D = 1024
KT = D // P
LAYERS = 2
PROMPT = 256
SAMPLES, SAMPLE_T = 8, 8
NT = PROMPT + SAMPLES * SAMPLE_T
TILES = 3
CH = 16
NCH = PROMPT // CH
MEM = 256
XH = 4
EXPERTS, GROUPS, EPG = 16, 4, 4
F = 512
ALPHA = (2 * LAYERS) ** 0.25
LN_EPS, RMS_EPS = 1e-5, 1e-6
GATE_NORM = 16.0
BIG = 1e30
RING = 3
NB = 512
GCH = 24
KV_BLOCKS = 2 * 4
IN_BLOCKS = (8, 6)
BLOCKS0 = KV_BLOCKS + IN_BLOCKS[0] + 6
BLOCKS1 = BLOCKS0 + IN_BLOCKS[1] + 6

MOE_ORDER = []
for _e in range(EPG):
    MOE_ORDER += [("gate", _e, 0), ("gate", _e, 1), ("up", _e, 0), ("up", _e, 1)]
    if _e:
        MOE_ORDER += [("down", _e - 1, 0), ("down", _e - 1, 1)]
MOE_ORDER += [("down", EPG - 1, 0), ("down", EPG - 1, 1)]
GU_LAST = [MOE_ORDER.index(("up", e, 1)) for e in range(EPG)]
T_AFTER = {GU_LAST[1] - 2: 0, GU_LAST[1] + 4: 1, GU_LAST[2] + 4: 2, GU_LAST[3] + 1: 3}


def mixer_shape(l):
    return (8, 128, 1, 1.0) if l == 0 else (4, 256, 2, 1.0 / GATE_NORM)


def first_block(l):
    return KV_BLOCKS if l == 0 else BLOCKS0


def block_kind(l, n):
    kinds = [("f", 2), ("q", 2), ("gate", 2), ("v", 2)] if l == 0 else [("q", 1), ("k", 1), ("gate", 2), ("v", 2)]
    for kind, count in kinds:
        if n < count:
            return kind, n
        n -= count


def at(static, groups, per):
    return static if groups is None else groups * per + static


def decoder_step(nc, a):
    with ExitStack() as ctx:
        def sb(name, shape, dt=F32):
            return ctx.enter_context(nc.sbuf_tensor(name, shape, dt))

        def sem(name):
            return ctx.enter_context(nc.semaphore(name))

        raw = sb("raw", [P, RING, 4, NB])
        w_hi = sb("w_hi", [P, RING, 4, NB], F32R)
        w_lo = sb("w_lo", [P, RING, 4, NB], F32R)
        x = sb("x", [P, TILES, D])
        xt_hi = sb("xt_hi", [P, KT, TILES * P], F32R)
        xt_lo = sb("xt_lo", [P, KT, TILES * P], F32R)
        ln_gb = sb("ln_gb", [P, 2, D])
        ident = sb("ident", [P, P])
        ones = sb("ones", [P, P])
        before = sb("before", [P, P])
        slot_no = sb("slot_no", [P, P])
        mask16 = sb("mask16", [P, P], U32)
        mask8 = sb("mask8", [P, 64], U32)
        mask_f = sb("mask_f", [P, P])
        carry = sb("carry", [P, NT])
        row_mod2 = sb("row_mod2", [P, 2])
        row_mod4 = sb("row_mod4", [P, 4])
        lb_rows = sb("lb_rows", [P, 3, 8])
        lb = sb("lb", [P, 8])
        one_m_lb = sb("one_m_lb", [P, 8])
        lb_tmp = sb("lb_tmp", [P, 8])
        gain_a = sb("gain_a", [P, 1])
        gain_b = sb("gain_b", [P, 2])
        b_gk = sb("b_gk", [P, 4])
        w_gk = sb("w_gk", [16, 512])
        w_lr = sb("w_lr", [P, KT, 16])
        lr_t = sb("lr_t", [16, NT])
        router = sb("router", [P, KT, EXPERTS])
        r_bias = sb("r_bias", [P, EXPERTS])
        g_base = sb("g_base", [P, GROUPS])
        e_rank = sb("e_rank", [P, EXPERTS])
        stats = sb("stats", [P, TILES, 12])
        mean_var = sb("mean_var", [P, TILES, 2])
        rstd = sb("rstd", [P, TILES])
        u_slot = sb("u_slot", [P, TILES])
        comb4 = sb("comb4", [P, TILES, EPG])
        n_iter = sb("n_iter", [1, 1], I32)
        ps = ctx.enter_context(nc.psum_tensor("ps", [P, 8, 512], F32))

        def stage(name, tensors):
            with ExitStack() as s:
                return {k: s.enter_context(nc.sbuf_tensor(f"{name}_{k}", shape, dt)) for k, (shape, dt) in tensors.items()}

        st_kv = stage("kv", {"mem": ([P, 2, D], F32), "out": ([P, 2, 2, NB], F32)})
        st_mix = []
        for l in range(LAYERS):
            H, V, VB, _ = mixer_shape(l)
            st_mix.append(stage(f"mix{l}", {
                "q": ([P, H, NT], F32), "k": ([P, H, NT], F32), "b": ([P, H, NT], F32),
                "g": ([P, 8, NT], F32), "v": ([P, TILES, D], F32),
                "s": ([P, 8, V], F32), "e": ([P, 2, 4, NT], F32), "t": ([P, 2, NT], F32),
                "dc": ([P, 2, NCH + SAMPLES], F32), "sc": ([P, TILES, P], F32),
                "kn": ([P, 2, 2, P], F32), "ks": ([P, 4, P], F32), "s0": ([P, SAMPLES, V], F32),
                "sq": ([P, VB, NT], F32), "rn": ([P, NT], F32)}))
        st_att = stage("att", {
            "q": ([P, 8, NT], F32), "kt": ([P, 2, 8, MEM], F32), "kn": ([P, 2, 2, D], F32),
            "vn": ([P, 2, 2, D], F32), "p": ([P, 2, XH, MEM], F32), "pt": ([P, 2, XH, PROMPT], F32),
            "pts": ([P, 2, XH, 64], F32), "sts": ([P, 2, XH, 64], F32),
            "mx": ([P, 3, XH], F32), "sum": ([P, 3, XH], F32), "rs": ([P, 3, XH], F32)})
        st_moe = stage("moe", {
            "xn_hi": ([P, TILES, D], F32R), "xn_lo": ([P, TILES, D], F32R),
            "xg_hi": ([P, KT, P], F32R), "xg_lo": ([P, KT, P], F32R),
            "y_hi": ([P, D], F32R), "y_lo": ([P, D], F32R),
            "pick": ([P, TILES, P], F32R), "pick_t": ([P, TILES * P], F32R), "cw": ([P, EPG], F32),
            "sil": ([P, F], F32), "h": ([P, 2, F], F32),
            "ht_hi": ([P, 2, 4, P], F32R), "ht_lo": ([P, 2, 4, P], F32R),
            "sc": ([P, TILES, EXPERTS], F32), "sel": ([P, TILES, EXPERTS], F32),
            "pair": ([P, TILES, GROUPS, 6], F32), "gs": ([P, TILES, GROUPS], F32),
            "gm": ([P, TILES], F32), "g": ([P, TILES, GROUPS], F32),
            "r1": ([P, TILES, EXPERTS], F32), "r2": ([P, TILES, EXPERTS], F32), "r3": ([P, TILES, EXPERTS], F32),
            "m1": ([P, TILES], F32), "pos": ([P, TILES, GROUPS], F32), "p2": ([P, TILES, GROUPS], F32),
            "mc": ([P, 1], F32), "mc2": ([P, 1], F32)})

        loaded = [sem(f"w_loaded{i}") for i in range(RING)]
        w_high = sem("w_high")
        w_low = sem("w_low")
        w_used = sem("w_used")
        evac = [sem("evac0"), sem("evac1")]
        xt_ps, xt_h, xt_l = sem("xt_ps"), sem("xt_h"), sem("xt_l")
        consts_in, consts = sem("consts_in"), sem("consts")
        mem_in, x_in, x_pad = sem("mem_in"), sem("x_in"), sem("x_pad")
        kv_out = [sem("kv_out0"), sem("kv_out1")]
        ln_in, ln_var, ln_rstd, ln_done = sem("ln_in"), sem("ln_var"), sem("ln_rstd"), sem("ln_done")
        dve_step, act_step, pool_step = sem("dve_step"), sem("act_step"), sem("pool_step")
        y_out = sem("y_out")
        mx_exp, mx_inv, mx_ln, mx_scan = sem("mx_exp"), sem("mx_inv"), sem("mx_ln"), sem("mx_scan")
        mx_lr, mx_lrc, mx_z = sem("mx_lr"), sem("mx_lrc"), sem("mx_z")
        hd_t, hd_e, hd_m = sem("hd_t"), sem("hd_e"), sem("hd_m")
        hd_sc, hd_tr = sem("hd_sc"), sem("hd_tr")
        hd_msk, hd_kn = sem("hd_msk"), sem("hd_kn")
        hd_u, hd_s = sem("hd_u"), sem("hd_s")
        hd_i = sem("hd_i")
        hd_su, hd_ss = sem("hd_su"), sem("hd_ss")
        hd_o, hd_sq, hd_ms, hd_ln, hd_r = sem("hd_o"), sem("hd_sq"), sem("hd_ms"), sem("hd_ln"), sem("hd_r")
        hd_y, hd_hi, hd_fin = sem("hd_y"), sem("hd_hi"), sem("hd_fin")
        s0_in, s0_out, s_out = sem("s0_in"), sem("s0_out"), sem("s_out")
        k_in, v_in = [sem("k_in0"), sem("k_in1")], [sem("v_in0"), sem("v_in1")]
        at_tr, at_ka, at_kv = sem("at_tr"), sem("at_ka"), sem("at_kv")
        at_sc, at_max, at_exp, at_p = sem("at_sc"), sem("at_max"), sem("at_exp"), sem("at_p")
        at_st, at_sts, at_sn = sem("at_st"), sem("at_sts"), sem("at_sn")
        at_pt, at_pte, at_pv, at_oh, at_ol = sem("at_pt"), sem("at_pte"), sem("at_pv"), sem("at_oh"), sem("at_ol")
        rt_ps, rt_e, rt_g, rt_pos, rt_n = sem("rt_ps"), sem("rt_e"), sem("rt_g"), sem("rt_pos"), sem("rt_n")
        mo = [{k: sem(f"mo{l}_{k}") for k in (
            "xh", "step", "p", "g", "pt", "ptc", "xgh", "xgl", "sil", "h", "t", "hth", "htl", "yh", "yl", "s", "add")}
            for l in range(LAYERS)]

        block = ctx.enter_context(nc.Block())

        def chunk_of(w, col, half):
            return w[half * 512:(half + 1) * 512, col:col + NB].rearrange("(k p) n -> p k n", p=P)

        def block_source(db):
            if db < KV_BLOCKS:
                return a["xattn_w_kv"][db // 4], (db % 4) * NB
            l = 0 if db < BLOCKS0 else 1
            n = db - first_block(l)
            if n < IN_BLOCKS[l]:
                kind, c = block_kind(l, n)
                if l == 0:
                    return a["hgrn_w_in"][0], {"q": 0, "f": 1024, "v": 2048, "gate": 3072}[kind] + c * NB
                return a["gla_w_in"][0], {"q": 0, "k": 512, "v": 1024, "gate": 2048}[kind] + c * NB
            n -= IN_BLOCKS[l]
            w = (a["hgrn_w_out" if l == 0 else "gla_w_out"][0], a["xattn_w_q"][l], a["xattn_w_o"][l])[n // 2]
            return w, (n % 2) * NB

        @block.sync
        def _(sp):
            def load(k, groups, src):
                if k >= RING:
                    sp.wait_ge(w_low, at(k - RING + 1, groups, GCH))
                sp.dma_start(raw[:, k % RING], src).then_inc(loaded[k % RING], 16)

            def dense(first, last, groups):
                for k in range(first, last):
                    w, col = block_source(k // 2)
                    load(k, groups, chunk_of(w, col, k % 2))

            def group(l, base, groups, g):
                for j, (what, e, half) in enumerate(MOE_ORDER):
                    w = a["moe_w_" + what][l]
                    expert = g * EPG + e
                    if isinstance(g, int):
                        w = w[expert]
                    else:
                        w = w[bass.ds(expert, 1)].rearrange("a r c -> (a r) c")
                    src = chunk_of(w, half * NB, 0) if what == "down" else chunk_of(w, 0, half)
                    load(base + j, groups, src)

            for k in range(3):
                w, col = block_source(k // 2)
                load(k, None, chunk_of(w, col, k % 2))
            sp.dma_start(st_kv["mem"][:, :, :], a["mem_prompt"][0].rearrange("(t p) c -> p t c", p=P)).then_inc(mem_in, 16)
            sp.dma_start(x[:, 0:2, :], a["x_prompt"][0].rearrange("(t p) c -> p t c", p=P)).then_inc(x_in, 16)
            sp.dma_start(x[0:64, 2, :], a["x_sample"].rearrange("b t c -> (b t) c")).then_inc(x_in, 16)
            groups = None
            done = 3
            for l in range(LAYERS):
                H, V, VB, _ = mixer_shape(l)
                m = st_mix[l]
                in_end = 2 * (first_block(l) + IN_BLOCKS[l])
                dense(done, in_end + 2 * RING, groups)
                done = in_end + 2 * RING
                s_in = a["state_hgrn" if l == 0 else "state_gla"][0]
                s_new = a["state_hgrn_sample" if l == 0 else "state_gla_sample"][0]
                s_fin = a["state_hgrn_prompt" if l == 0 else "state_gla_prompt"][0, 0]
                h0 = l * 8
                for h in range(H):
                    if h == 0:
                        sp.wait_ge(mx_scan, l * 8 + 1)
                    else:
                        sp.wait_ge(s0_out, 16 * (h0 + h))
                    sp.dma_start(m["s0"][:, :, :], s_in[:, h].rearrange("b k v -> k b v")).then_inc(s0_in, 16)
                    sp.wait_ge(hd_s, NCH * (h0 + h + 1))
                    sp.dma_start(s_fin[h], m["s"][:, (NCH - 1) % 8, :]).then_inc(s_out, 16)
                    sp.wait_ge(hd_ss, SAMPLES * (h0 + h + 1))
                    sp.dma_start(s_new[:, h].rearrange("b k v -> k b v"), m["s0"][:, :, :]).then_inc(s0_out, 16)
                last = 2 * (BLOCKS0 if l == 0 else BLOCKS1)
                dense(done, last, groups)
                done = last
                group(l, last, groups, 0)
                sp.wait_ge(rt_n, l + 1)
                n = sp.value_load(n_iter[0:1, 0:1], min_val=4, max_val=12)
                with sp.Fori(1, n) as i:
                    group(l, last, i if groups is None else groups + i, i % GROUPS)
                groups = n
            sp.wait_ge(s_out, 16 * 12)
            sp.wait_ge(s0_out, 16 * 12)

        @block.gpsimd
        def _(pool):
            steps = [0]

            def link(ins):
                steps[0] += 1
                ins.then_inc(pool_step, 1)
                pool.wait_ge(pool_step, steps[0])

            small = [(gain_a[:, :], a["hgrn_norm_g"].rearrange("o p -> p o")),
                     (gain_b[:, :], a["gla_norm_g"].rearrange("o (c p) -> p (o c)", p=P)),
                     (b_gk[:, :], a["gla_b_gk2"].rearrange("o (c p) -> p (o c)", p=P)),
                     (w_gk[:, :], a["gla_w_gk2"][0]),
                     (w_lr[:, :, :], a["gla_w_in"][0][:, 3072:3088].rearrange("(k p) n -> p k n", p=P)),
                     (router[:, :, :], a["router_w"].rearrange("(k p) n -> p k n", p=P)),
                     (r_bias[:, :], a["router_bias"].partition_broadcast(P))]
            small += [(lb_rows[:, r, :], a["hgrn_lb_logits"][r].rearrange("(h p) -> p h", p=P)) for r in range(3)]
            with nc.allow_non_contiguous_dma(reason="a few hundred words, once"):
                for dst, src in small:
                    pool.dma_start(dst, src).then_inc(consts_in, 16)

            def select(t, fill, base, pattern, mult, op=ALU.is_ge):
                link(nc.gpsimd.affine_select(out=t, in_=t, compare_op=op, fill=fill, base=base,
                                             pattern=pattern, channel_multiplier=mult))
            link(nc.gpsimd.memset(ident[:], 0.0))
            select(ident[:], 1.0, 0, [[-1, P]], 1, ALU.not_equal)
            nc.gpsimd.memset(ones[:], 1.0)
            link(nc.gpsimd.memset(before[:], 1.0))
            select(before[:], 0.0, -1, [[1, P]], -1)
            link(nc.gpsimd.iota(slot_no[:], [[1, P]], base=0, channel_multiplier=0, allow_small_or_imprecise_dtypes=True))
            link(nc.gpsimd.iota(g_base[:], [[P, GROUPS]], base=1, channel_multiplier=0, allow_small_or_imprecise_dtypes=True))
            link(nc.gpsimd.iota(e_rank[:], [[-1, EXPERTS]], base=EXPERTS, channel_multiplier=0, allow_small_or_imprecise_dtypes=True))
            link(nc.gpsimd.memset(mask_f[:], 1.0))
            view = mask_f[:].rearrange("p (c i) -> p c i", i=CH)
            select(view, 0.0, 0, [[CH, P // CH], [1, CH]], -1)
            select(view, 0.0, 0, [[-CH, P // CH], [0, CH]], 1)
            link(nc.gpsimd.tensor_copy(mask16[:], mask_f[:]))
            link(nc.gpsimd.memset(mask_f[:], 1.0))
            view = mask_f[:, 0:64].rearrange("p (c i) -> p c i", i=8)
            select(view, 0.0, 0, [[8, 8], [1, 8]], -1)
            select(view, 0.0, 0, [[-8, 8], [0, 8]], 1)
            link(nc.gpsimd.tensor_copy(mask8[:], mask_f[:, 0:64]))
            link(nc.gpsimd.memset(carry[:], 1.0))
            link(nc.gpsimd.memset(carry[:, 0:PROMPT].rearrange("p (c i) -> p c i", i=CH)[:, :, 0:1], 0.0))
            link(nc.gpsimd.memset(carry[:, PROMPT:NT].rearrange("p (c i) -> p c i", i=8)[:, :, 0:1], 0.0))
            link(nc.gpsimd.memset(mask_f[:], 1.0))
            v8 = mask_f[:, 0:8].rearrange("p (r e) -> p e r", e=2)
            select(mask_f[:, 0:8], 0.0, 0, [[-16, 8]], 1)
            select(mask_f[:, 0:8], 0.0, 15, [[16, 8]], -1)
            select(mask_f[:, 16:32], 0.0, 0, [[-8, 16]], 1)
            select(mask_f[:, 16:32], 0.0, 7, [[8, 16]], -1)
            nc.gpsimd.sem_inc(consts, 1)

            for db in range(KV_BLOCKS):
                par, l, c = db % 2, db // 4, db % 4
                pool.wait_ge(evac[par], db // 2 + 1)
                dst = a["mem_k_prompt" if c < 2 else "mem_v_prompt"][l, 0].rearrange("(t p) h d -> p t (h d)", p=P)
                pool.dma_start(dst[:, :, (c % 2) * NB:(c % 2 + 1) * NB], st_kv["out"][:, par]).then_inc(kv_out[par], 16)

            def load_ln(q):
                if q:
                    pool.wait_ge(ln_done, TILES * q)
                pool.dma_start(ln_gb[:, 0, :], a["ln_g"][q // 3, q % 3].partition_broadcast(P)).then_inc(ln_in, 16)
                pool.dma_start(ln_gb[:, 1, :], a["ln_b"][q // 3, q % 3].partition_broadcast(P)).then_inc(ln_in, 16)

            def head_gates(l, h):
                H, V, VB, _ = mixer_shape(l)
                m, n = st_mix[l], l * 8 + h
                b = m["b"][:, h, :]
                bp, bs = b[:, 0:PROMPT].rearrange("p (c i) -> p c i", i=CH), b[:, PROMPT:NT].rearrange("p (c i) -> p c i", i=8)
                pool.wait_ge(mx_scan, n + 1)
                if h:
                    pool.wait_ge(hd_e, n)
                for r, (lo, hi) in enumerate(((CH // 2, 4), (CH - 1, 7))):
                    tp = m["t"][:, r, 0:PROMPT].rearrange("p (c i) -> p c i", i=CH)
                    ts = m["t"][:, r, PROMPT:NT].rearrange("p (c i) -> p c i", i=8)
                    rp, rs = bp[:, :, lo:lo + 1].to_broadcast([P, NCH, CH]), bs[:, :, hi:hi + 1].to_broadcast([P, 8, 8])
                    if r == 0:
                        nc.gpsimd.tensor_tensor(tp, bp, rp, ALU.subtract)
                        nc.gpsimd.tensor_tensor(ts, bs, rs, ALU.subtract)
                    else:
                        nc.gpsimd.tensor_tensor(tp, rp, bp, ALU.subtract)
                        nc.gpsimd.tensor_tensor(ts, rs, bs, ALU.subtract).then_inc(hd_t, 1)

            def head_products(l, h):
                m, n = st_mix[l], l * 8 + h
                pool.wait_ge(hd_e, n + 1)
                e = m["e"][:, h % 2]
                for r, src in enumerate(("q", "k", "q", "k")):
                    ins = nc.gpsimd.tensor_tensor(e[:, r, :], e[:, r, :], m[src][:, h, :], ALU.mult)
                ins.then_inc(hd_m, 1)

            for l in range(LAYERS):
                H, V, VB, _ = mixer_shape(l)
                load_ln(3 * l)
                head_gates(l, 0)
                for h in range(H):
                    if h + 1 < H:
                        head_gates(l, h + 1) if False else None
                    head_products(l, h)
                    if h + 1 < H:
                        head_gates(l, h + 1)
                pool.wait_ge(hd_fin, l * 8 + H)
                pool.wait_ge(s0_out, 16 * (l * 8 + H))
                pool.wait_ge(s_out, 16 * (l * 8 + H))
                if l == 0:
                    for par in range(2):
                        pool.wait_ge(kv_out[par], 16 * KV_BLOCKS // 2)
                order = [("k", 0), ("v", 0)] + [("k", n) for n in range(1, 9)] + [("v", n) for n in range(1, 9)]
                for kind, n in order:
                    c = 9 * l + n
                    par = c % 2
                    if n >= 2 and kind == "k":
                        pool.wait_ge(at_tr, 4 * (c - 1))
                    if n >= 2 and kind == "v":
                        pool.wait_ge(at_pv, c - 1)
                    if n == 0:
                        src = a["mem_k_prompt" if kind == "k" else "mem_v_prompt"][l, 0]
                    else:
                        src = a["cache_mem_" + kind][l, n - 1]
                    pool.dma_start(st_att[kind + "n"][:, par], src.rearrange("(t p) h d -> p t (h d)", p=P))\
                        .then_inc((k_in if kind == "k" else v_in)[par], 16)
                load_ln(3 * l + 1)
                load_ln(3 * l + 2)
                if l == LAYERS - 1:
                    pool.wait_ge(ln_done, TILES * 6)
                    pool.dma_start(a["y_prompt"][0].rearrange("(t p) c -> p t c", p=P), x[:, 0:2, :]).then_inc(y_out, 16)
                    pool.dma_start(a["y_sample"].rearrange("b t c -> (b t) c"), x[0:64, 2, :]).then_inc(y_out, 16)
                    pool.wait_ge(y_out, 32)

        @block.scalar
        def _(act):
            splits = [0]

            def split(k, groups):
                act.wait_ge(loaded[k % RING], at(16 * (k // RING + 1), groups, 16 * GCH // RING))
                if k >= RING:
                    act.wait_ge(w_used, at(k - RING + 1, groups, GCH))
                nc.scalar.activation(w_hi[:, k % RING], raw[:, k % RING], ACT.Copy).then_inc(w_high, 1)

            def split_ahead(db, groups):
                limit = 2 * (BLOCKS0 if db < BLOCKS0 else BLOCKS1)
                while splits[0] < min(2 * db + 5, limit):
                    split(splits[0], groups)
                    splits[0] += 1

            def block_out(db, groups, out, ins, func, **kw):
                split_ahead(db, groups)
                act.wait_ge(w_used, at(2 * db + 2, groups, GCH))
                return nc.scalar.activation(out, ins, func, **kw)

            def transposed(u, tiles):
                for kt in range(KT):
                    act.wait_ge(xt_ps, 8 * u + kt + 1)
                    nc.scalar.activation(xt_hi[:, kt, 0:tiles * P], ps[:, kt % 4, 0:tiles * P], ACT.Copy).then_inc(xt_h, 1)

            def layer_norm(q):
                act.wait_ge(ln_var, q + 1)
                nc.scalar.activation(rstd[:], rstd[:], ACT.Ln).then_inc(act_step, 1)
                act.wait_ge(act_step, q + 1)
                nc.scalar.activation(rstd[:], rstd[:], ACT.Exp, scale=-0.5).then_inc(ln_rstd, 1)

            def sigmoid_parts(db, groups, dst):
                block_out(db, groups, dst, ps[:, 4 * (db % 2):4 * (db % 2) + 4, 0:NT], ACT.Exp, scale=-1.0)\
                    .then_inc(mx_exp, 1)

            def head(l, h):
                H, V, VB, gs = mixer_shape(l)
                m, n = st_mix[l], l * 8 + h
                if h < 2:
                    pass
                else:
                    act.wait_ge(hd_o, n - 1)
                act.wait_ge(hd_t, n + 1)
                e, t, b = m["e"][:, h % 2], m["t"], m["b"][:, h, :]
                nc.scalar.activation(e[:, 0, :], t[:, 0, :], ACT.Exp, scale=gs)
                nc.scalar.activation(e[:, 1, :], t[:, 0, :], ACT.Exp, scale=-gs)
                nc.scalar.activation(e[:, 2, :], b, ACT.Exp, scale=gs)
                nc.scalar.activation(e[:, 3, :], t[:, 1, :], ACT.Exp, scale=gs)
                nc.scalar.activation(m["dc"][:, h % 2, 0:NCH], b[:, CH - 1:PROMPT:CH], ACT.Exp, scale=gs)
                nc.scalar.activation(m["dc"][:, h % 2, NCH:NCH + 8], b[:, PROMPT + 7:NT:8], ACT.Exp, scale=gs).then_inc(hd_e, 1)

            def head_keys(l, h):
                m, n = st_mix[l], l * 8 + h
                act.wait_ge(hd_tr, n + 1)
                kp = ps[:, 1, 0:PROMPT].rearrange("p (t k) -> p t k", t=2)
                for e in range(2):
                    nc.scalar.activation(m["kn"][:, :, e, :], kp, ACT.Copy, scale=row_mod2[:, e:e + 1])
                for r in range(4):
                    ins = nc.scalar.activation(m["ks"][0:64, r, :], ps[0:64, 1, PROMPT:PROMPT + P], ACT.Copy,
                                               scale=row_mod4[0:64, r:r + 1])
                ins.then_inc(hd_kn, 1)

            def head_norm(l, h):
                H, V, VB, gs = mixer_shape(l)
                m, n = st_mix[l], l * 8 + h
                act.wait_ge(hd_o, n + 1)
                nc.scalar.activation(m["sq"][:], ps[:, 6:6 + VB, 0:NT], ACT.Square).then_inc(hd_sq, 1)
                act.wait_ge(hd_ms, 2 * (n + 1))
                nc.scalar.activation(m["rn"][:], m["rn"][:], ACT.Ln).then_inc(hd_ln, 1)
                act.wait_ge(hd_ln, n + 1)
                nc.scalar.activation(m["rn"][:], m["rn"][:], ACT.Exp, scale=-0.5).then_inc(hd_r, 1)
                act.wait_ge(hd_y, n + 1)
                nc.scalar.activation(xt_hi[:, h * VB:(h + 1) * VB, 0:NT], m["sq"][:], ACT.Copy).then_inc(hd_hi, 1)

            nc.scalar.preload_act_table_set("natural_log_exp_and_others")
            split_ahead(-1, None)
            transposed(0, 2)
            for db in range(KV_BLOCKS):
                par = db % 2
                if db >= 2:
                    act.wait_ge(kv_out[par], 16 * (db // 2))
                block_out(db, None, st_kv["out"][:, par], ps[:, 4 * par:4 * par + 2, :], ACT.Copy).then_inc(evac[par], 1)
            transposed(1, TILES)
            act.wait_ge(consts, 4)
            nc.scalar.activation(lb_rows[:], lb_rows[:], ACT.Exp).then_inc(consts, 1)
            groups = None
            for l in range(LAYERS):
                H, V, VB, gs = mixer_shape(l)
                m = st_mix[l]
                if l == 0:
                    for par in range(2):
                        act.wait_ge(kv_out[par], 16 * KV_BLOCKS // 2)
                for nb in range(IN_BLOCKS[l]):
                    db = first_block(l) + nb
                    par = db % 2
                    kind, c = block_kind(l, nb)
                    four = ps[:, 4 * par:4 * par + 4, 0:NT]
                    e_dst = m["e"][:, c % 2]
                    if kind == "f":
                        sigmoid_parts(db, groups, m["b"][:, 4 * c:4 * c + 4, :])
                    elif kind == "q" and l == 0:
                        sigmoid_parts(db, groups, e_dst)
                    elif kind == "gate":
                        if l == 0:
                            act.wait_ge(mx_inv, 3 + c)
                        elif c == 1:
                            act.wait_ge(mx_inv, 9)
                        sigmoid_parts(db, groups, e_dst)
                    elif kind in ("q", "k"):
                        block_out(db, groups, m[kind][:], four, ACT.Copy,
                                  scale=float(P) ** -0.5 if kind == "q" else 1.0).then_inc(evac[par], 1)
                    else:
                        block_out(db, groups, m["v"][:, :, c * NB:(c + 1) * NB], ps[:, 4 * par:4 * par + 3, :], ACT.Copy)\
                            .then_inc(evac[par], 1)
                    if kind == "f":
                        pass
                    if l == 0 and kind == "q":
                        act.wait_ge(mx_inv, c + 1)
                        nc.scalar.activation(m["b"][:, 4 * c:4 * c + 4, :], m["b"][:, 4 * c:4 * c + 4, :], ACT.Ln).then_inc(mx_ln, 1)
                    if l == 1 and kind == "k":
                        act.wait_ge(mx_lr, 1)
                        nc.scalar.activation(lr_t[:], ps[0:16, 3, 0:NT], ACT.Copy).then_inc(mx_lrc, 1)
                        for hh in range(4):
                            act.wait_ge(mx_z, hh + 1)
                            nc.scalar.activation(m["b"][:, hh, :], ps[:, hh % 2, 0:NT], ACT.Abs, bias=b_gk[:, hh:hh + 1]).then_inc(mx_lrc, 1)
                        act.wait_ge(mx_lrc, 5)
                        nc.scalar.activation(m["b"][:], m["b"][:], ACT.Exp, scale=-1.0).then_inc(mx_lrc, 1)
                        act.wait_ge(mx_lrc, 6)
                        nc.scalar.activation(m["b"][:], m["b"][:], ACT.Ln, bias=1.0).then_inc(mx_ln, 1)
                head(l, 0)
                for h in range(H):
                    head_keys(l, h)
                    if h + 1 < H:
                        head(l, h + 1)
                    head_norm(l, h)
                db = first_block(l) + IN_BLOCKS[l]
                split_ahead(db, groups)
                split_ahead(db + 1, groups)
                layer_norm(3 * l)
                transposed(2 + 3 * l, TILES)
                for c in range(2):
                    d2 = db + 2 + c
                    block_out(d2, groups, st_att["q"][:, 4 * c:4 * c + 4, :], ps[:, 4 * (d2 % 2):4 * (d2 % 2) + 4, 0:NT], ACT.Copy)\
                        .then_inc(evac[d2 % 2], 1)
                split_ahead(db + 3, groups)

                def keys_out(n):
                    c = 9 * l + n
                    for s in (0, 2):
                        act.wait_ge(at_tr, 4 * c + s + 1)
                        if n >= 2:
                            act.wait_ge(at_sc, c - 1)
                        nc.scalar.activation(st_att["kt"][:, c % 2, 2 * s:2 * s + 2, :], ps[:, 0, :].rearrange("p (b m) -> p b m", b=2),
                                             ACT.Copy).then_inc(at_ka, 1)

                def exps(t, rows, banks):
                    act.wait_ge(at_max, 3 * l + t + 1)
                    s = ps[0:rows, banks:banks + 2, :].rearrange("p a (b m) -> p (a b) m", b=2)
                    for hh in range(XH):
                        ins = nc.scalar.activation(st_att["p"][0:rows, t % 2, hh, :], s[:, hh, :], ACT.Exp,
                                                   bias=st_att["mx"][0:rows, t, hh:hh + 1], scale=float(D // XH) ** -0.5,
                                                   accum_out=st_att["sum"][0:rows, t, hh:hh + 1])
                    ins.then_inc(at_exp, 1)

                keys_out(0)
                exps(0, P, 4)
                exps(1, P, 6)
                for n in range(1, 9):
                    keys_out(n)
                act.wait_ge(at_st, l + 1)
                nc.scalar.activation(st_att["sts"][:].rearrange("p a b c -> p (a b c)"), ps[:, 2, :], ACT.Copy).then_inc(at_sts, 1)
                for r in range(4):
                    act.wait_ge(at_pt, 5 * l + r + 1)
                    nc.scalar.activation(st_att["pt"][:, r % 2, :, (r // 2) * P:(r // 2 + 1) * P],
                                         ps[:, 3 if r % 2 else 2, :].rearrange("p (h q) -> p h q", h=XH), ACT.Copy).then_inc(at_pte, 1)
                act.wait_ge(at_pv, 9 * l + 1)
                nc.scalar.activation(xt_hi[:, :, 0:PROMPT], ps[:, 4:8, :].rearrange("p a (b q) -> p (a b) q", b=2), ACT.Copy).then_inc(at_oh, 1)
                exps(2, 64, 0)
                act.wait_ge(at_pt, 5 * l + 5)
                nc.scalar.activation(st_att["pts"][:].rearrange("p a b c -> p (a b c)"), ps[:, 3, :], ACT.Copy).then_inc(at_pte, 1)
                act.wait_ge(at_pv, 9 * l + 9)
                nc.scalar.activation(xt_hi[:, :, PROMPT:NT], ps[:, 2, :].rearrange("p (b q) -> p b q", b=8), ACT.Copy).then_inc(at_oh, 1)
                split_ahead(db + 4, groups)
                split_ahead(db + 5, groups)
                layer_norm(3 * l + 1)
                transposed(3 + 3 * l, TILES)
                m, s = st_moe, mo[l]
                nc.scalar.activation(m["xn_hi"][:], x[:], ACT.Copy).then_inc(s["xh"], 1)
                act.wait_ge(rt_ps, l + 1)
                nc.scalar.activation(m["sc"][:].rearrange("p t e -> p (t e)"), ps[:, 4, 0:TILES * EXPERTS], ACT.Exp, scale=-1.0).then_inc(rt_e, 1)
                act.wait_ge(rt_n, l + 1)
                n = act.value_load(n_iter[0:1, 0:1], min_val=4, max_val=12)
                base = splits[0]
                with act.Fori(0, n) as i:
                    g = i if groups is None else groups + i
                    for j in range(3):
                        split(base + j, g)
                    act.wait_ge(s["pt"], i + 1)
                    nc.scalar.activation(m["pick_t"][:], ps[:, 7, 0:TILES * P], ACT.Copy)
                    nc.scalar.activation(m["cw"][:], ps[:, 7, TILES * P:TILES * P + EPG], ACT.Copy).then_inc(s["ptc"], 1)
                    act.wait_ge(s["g"], i + 1)
                    nc.scalar.activation(m["xg_hi"][:].rearrange("p (a k) s -> p a (k s)", a=2), ps[:, 4:6, :], ACT.Copy).then_inc(s["xgh"], 1)
                    for j in range(3, GCH):
                        split(base + j, g)
                        for e in range(EPG):
                            if j == GU_LAST[e] + 3:
                                act.wait_ge(w_used, at(base + GU_LAST[e] + 1, g, GCH))
                                act.wait_ge(s["h"], i * EPG + e + 1)
                                nc.scalar.activation(m["sil"][:], ps[:, 2 * (e % 2), :], ACT.Silu).then_inc(s["sil"], 1)
                        if j - 3 in T_AFTER:
                            e = T_AFTER[j - 3]
                            act.wait_ge(s["t"], i * EPG + e + 1)
                            nc.scalar.activation(m["ht_hi"][:, e % 2], ps[:, 6, :].rearrange("p (k s) -> p k s", k=4), ACT.Copy).then_inc(s["hth"], 1)
                    act.wait_ge(w_used, at(base + GCH, g, GCH))
                    nc.scalar.activation(m["y_hi"][:].rearrange("p (a c) -> p a c", a=2), ps[:, 4:6, :], ACT.Copy).then_inc(s["yh"], 1)
                groups = n
                nc.scalar.preload_act_table_set("natural_log_exp_and_others")
                layer_norm(3 * l + 2)
                if l == 0:
                    transposed(4, TILES)

        @block.vector
        def _(dve):
            splits, steps = [0], [0]

            def link(ins):
                steps[0] += 1
                ins.then_inc(dve_step, 1)
                dve.wait_ge(dve_step, steps[0])

            def split(k, groups):
                dve.wait_ge(w_high, at(k + 1, groups, GCH))
                nc.vector.tensor_tensor(w_lo[:, k % RING], raw[:, k % RING], w_hi[:, k % RING].bitcast(F32), ALU.subtract).then_inc(w_low, 1)

            def split_ahead(db, groups):
                limit = 2 * (BLOCKS0 if db < BLOCKS0 else BLOCKS1)
                while splits[0] < min(2 * db + 5, limit):
                    split(splits[0], groups)
                    splits[0] += 1

            def block_done(db, groups):
                split_ahead(db, groups)
                dve.wait_ge(w_used, at(2 * db + 2, groups, GCH))

            def transposed(u, tiles):
                for kt in range(KT):
                    dve.wait_ge(xt_h, 8 * u + kt + 1)
                    nc.vector.tensor_tensor(xt_lo[:, kt, 0:tiles * P], ps[:, kt % 4, 0:tiles * P],
                                            xt_hi[:, kt, 0:tiles * P].bitcast(F32), ALU.subtract).then_inc(xt_l, 1)

            def add_block(db, groups, c):
                block_done(db, groups)
                par = db % 2
                for t in range(TILES):
                    cols = x[:, t, c * NB:(c + 1) * NB]
                    ins = nc.vector.scalar_tensor_tensor(out=cols, in0=cols, scalar=ALPHA, in1=ps[:, 4 * par + t, :],
                                                         op0=ALU.mult, op1=ALU.add)
                ins.then_inc(evac[par], 1)
                dve.wait_ge(evac[par], db // 2 + 1)

            def layer_norm(q):
                for t in range(TILES):
                    for c in range(2):
                        ins = nc.vector.bn_stats(stats[:, t, 6 * c:6 * c + 6], x[:, t, c * NB:(c + 1) * NB])
                link(ins)
                for t in range(TILES):
                    ins = nc.vector.bn_aggr(mean_var[:, t, :], stats[:, t, :])
                link(ins)
                nc.vector.tensor_scalar(rstd[:], mean_var[:, :, 1], LN_EPS, None, ALU.add).then_inc(ln_var, 1)
                dve.wait_ge(ln_rstd, q + 1)
                dve.wait_ge(ln_in, 32 * (q + 1))
                for t in range(TILES):
                    link(nc.vector.tensor_scalar(x[:, t, :], x[:, t, :], mean_var[:, t, 0:1], rstd[:, t:t + 1], ALU.subtract, ALU.mult))
                    link(nc.vector.tensor_tensor(x[:, t, :], x[:, t, :], ln_gb[:, 0, :], ALU.mult))
                    nc.vector.tensor_tensor(x[:, t, :], x[:, t, :], ln_gb[:, 1, :], ALU.add).then_inc(ln_done, 1)
                dve.wait_ge(ln_done, TILES * (q + 1))

            def inverse(t):
                link(nc.vector.tensor_scalar(t, t, 1.0, None, ALU.add))
                link(nc.vector.reciprocal(t, t))

            nc.vector.memset(x[64:P, 2, :], 0.0).then_inc(x_pad, 1)
            dve.wait_ge(consts, 1)
            link(nc.vector.tensor_tensor(row_mod2[:], mask_f[:, 0:2], mask_f[:, 2:4], ALU.add))
            link(nc.vector.tensor_tensor(row_mod2[:], row_mod2[:], mask_f[:, 4:6], ALU.add))
            link(nc.vector.tensor_tensor(row_mod2[:], row_mod2[:], mask_f[:, 6:8], ALU.add))
            link(nc.vector.tensor_tensor(row_mod4[:], mask_f[:, 16:20], mask_f[:, 20:24], ALU.add))
            dve.wait_ge(consts_in, 160)
            nc.vector.tensor_tensor(lb_tmp[:], lb_rows[:, 0, :], lb_rows[:, 1, :], ALU.max).then_inc(consts, 1)
            dve.wait_ge(consts, 2)
            nc.vector.tensor_tensor(lb_tmp[:], lb_tmp[:], lb_rows[:, 2, :], ALU.max).then_inc(consts, 1)
            dve.wait_ge(consts, 3)
            nc.vector.tensor_tensor(lb_rows[:], lb_rows[:], lb_tmp[:].unsqueeze(1).to_broadcast([P, 3, 8]), ALU.subtract).then_inc(consts, 1)
            split_ahead(-1, None)
            transposed(0, 2)
            for db in range(KV_BLOCKS):
                split_ahead(db, None)
            transposed(1, TILES)
            dve.wait_ge(consts, 5)
            link(nc.vector.tensor_tensor(lb_tmp[:], lb_rows[:, 0, :], lb_rows[:, 1, :], ALU.add))
            link(nc.vector.tensor_tensor(lb_tmp[:], lb_tmp[:], lb_rows[:, 2, :], ALU.add))
            link(nc.vector.reciprocal(lb_tmp[:], lb_tmp[:]))
            link(nc.vector.tensor_tensor(lb[:], lb_rows[:, 0, :], lb_tmp[:], ALU.mult))
            link(nc.vector.tensor_scalar(one_m_lb[:], lb[:], -1.0, 1.0, ALU.mult, ALU.add))
            groups = None
            for l in range(LAYERS):
                H, V, VB, gs = mixer_shape(l)
                m = st_mix[l]
                exps_seen = 6 * l
                if l == 0:
                    for par in range(2):
                        dve.wait_ge(kv_out[par], 16 * KV_BLOCKS // 2)
                nc.vector.memset(m["sc"][:], 0.0)
                for nb in range(IN_BLOCKS[l]):
                    db = first_block(l) + nb
                    par = db % 2
                    kind, c = block_kind(l, nb)
                    split_ahead(db, groups)
                    four = ps[:, 4 * par:4 * par + 4, 0:NT]
                    if kind == "f":
                        exps_seen += 1
                        dve.wait_ge(mx_exp, exps_seen)
                        b4 = m["b"][:, 4 * c:4 * c + 4, :]
                        nc.vector.engine_nop().then_inc(evac[par], 1)
                        inverse(b4)
                        for hh in range(4 * c, 4 * c + 4):
                            ins = nc.vector.tensor_scalar(m["b"][:, hh, :], m["b"][:, hh, :], one_m_lb[:, hh:hh + 1], lb[:, hh:hh + 1], ALU.mult, ALU.add)
                        link(ins)
                        nc.vector.tensor_scalar(m["k"][:, 4 * c:4 * c + 4, :], b4, -1.0, 1.0, ALU.mult, ALU.add).then_inc(mx_inv, 1)
                    elif kind == "q" and l == 0:
                        exps_seen += 1
                        dve.wait_ge(mx_exp, exps_seen)
                        inverse(m["e"][:, c % 2])
                        for hh in range(4):
                            ins = nc.vector.scalar_tensor_tensor(out=m["q"][:, 4 * c + hh, :], in0=ps[:, 4 * par + hh, 0:NT], scalar=float(P) ** -0.5,
                                                                 in1=m["e"][:, c % 2, hh, :], op0=ALU.mult, op1=ALU.mult)
                        link(ins)
                        nc.vector.engine_nop().then_inc(evac[par], 1)
                        nc.vector.engine_nop().then_inc(mx_inv, 1)
                    elif kind == "gate":
                        exps_seen += 1
                        dve.wait_ge(mx_exp, exps_seen)
                        inverse(m["e"][:, c % 2])
                        for hh in range(4):
                            gain = gain_a[:, 0:1] if l == 0 else gain_b[:, hh % 2:hh % 2 + 1]
                            ins = nc.vector.scalar_tensor_tensor(out=m["g"][:, 4 * c + hh, :], in0=ps[:, 4 * par + hh, 0:NT], scalar=gain,
                                                                 in1=m["e"][:, c % 2, hh, :], op0=ALU.mult, op1=ALU.mult)
                        link(ins)
                        nc.vector.engine_nop().then_inc(evac[par], 1)
                    elif kind == "k" and l == 1:
                        for hh in range(4):
                            dve.wait_ge(mx_lrc, hh + 2)
                            ins = nc.vector.tensor_scalar(m["e"][:, 1, hh, :], ps[:, hh % 2, 0:NT], b_gk[:, hh:hh + 1], 0.0, ALU.add, ALU.min)
                            ins.then_inc(mx_inv, 1)
                        dve.wait_ge(mx_inv, 4 + 4)
                        dve.wait_ge(mx_ln, 3)
                        link(nc.vector.scalar_tensor_tensor(out=m["b"][:], in0=m["b"][:], scalar=-1.0, in1=m["e"][:, 1], op0=ALU.mult, op1=ALU.add))
                        nc.vector.engine_nop().then_inc(mx_inv, 1)
                    if l == 0 and kind == "v" and c == 0:
                        dve.wait_ge(mx_ln, 2)
                    if kind == "v" and c == 0:
                        for hh in range(H):
                            nc.vector.tensor_tensor_scan(m["b"][:, hh, :], carry[:], m["b"][:, hh, :], 0.0, ALU.mult, ALU.add).then_inc(mx_scan, 1)
                        if l == 1:
                            for _z in range(0):
                                pass
                for h in range(H):
                    n = l * 8 + h
                    dve.wait_ge(hd_sc, n + 1)
                    for t in range(2):
                        nc.vector.copy_predicated(m["sc"][:, t, :], mask16[:], ps[:, 0, t * P:(t + 1) * P])
                    nc.vector.copy_predicated(m["sc"][0:64, 2, 0:64], mask8[0:64, :], ps[0:64, 0, PROMPT:PROMPT + 64]).then_inc(hd_msk, 1)
                    dc = m["dc"][:, h % 2]

                    def new_state(c):
                        dve.wait_ge(hd_u, NCH // 2 * n + c // 2 + 1)
                        u = ps[:, 2 + (c % 8) // 2, (c % 2) * V:(c % 2 + 1) * V]
                        if c >= 8:
                            dve.wait_ge(hd_i, 15 * n + c - 8 + 1)
                        if c == 7 and h:
                            dve.wait_ge(s_out, 16 * n)
                        if c == 0:
                            nc.vector.tensor_copy(m["s"][:, 0, :], u).then_inc(hd_s, 1)
                        else:
                            dve.wait_ge(hd_s, NCH * n + c)
                            nc.vector.scalar_tensor_tensor(out=m["s"][:, c % 8, :], in0=m["s"][:, (c - 1) % 8, :], scalar=dc[:, c:c + 1],
                                                           in1=u, op0=ALU.mult, op1=ALU.add).then_inc(hd_s, 1)
                    for c in range(NCH):
                        new_state(c)
                    dve.wait_ge(s0_in, 16 * (n + 1))
                    for bb in range(SAMPLES):
                        dve.wait_ge(hd_su, SAMPLES // 2 * n + bb // 2 + 1)
                        u = ps[:, 2 + bb // 2, (bb % 2) * V:(bb % 2 + 1) * V]
                        nc.vector.scalar_tensor_tensor(out=m["s0"][:, bb, :], in0=m["s0"][:, bb, :], scalar=dc[:, NCH + bb:NCH + bb + 1],
                                                       in1=u, op0=ALU.mult, op1=ALU.add).then_inc(hd_ss, 1)
                    dve.wait_ge(hd_ms, 2 * n + 1)
                    nc.vector.tensor_scalar(m["rn"][:], ps[:, 1, 0:NT], 1.0 / V, RMS_EPS, ALU.mult, ALU.add).then_inc(hd_ms, 1)
                    link(nc.vector.tensor_tensor(m["sq"][:], ps[:, 6:6 + VB, 0:NT], m["g"][:, h * VB:(h + 1) * VB, :], ALU.mult))
                    dve.wait_ge(hd_r, n + 1)
                    rb = m["rn"][:].unsqueeze(1).to_broadcast([P, VB, NT])
                    nc.vector.tensor_tensor(m["sq"][:], m["sq"][:], rb, ALU.mult).then_inc(hd_y, 1)
                    dve.wait_ge(hd_hi, n + 1)
                    nc.vector.tensor_tensor(xt_lo[:, h * VB:(h + 1) * VB, 0:NT], m["sq"][:],
                                            xt_hi[:, h * VB:(h + 1) * VB, 0:NT].bitcast(F32), ALU.subtract).then_inc(hd_fin, 1)
                if l == 1:
                    nc.vector.engine_nop().then_inc(hd_y, 1)
                db = first_block(l) + IN_BLOCKS[l]
                add_block(db, groups, 0)
                add_block(db + 1, groups, 1)
                layer_norm(3 * l)
                transposed(2 + 3 * l, TILES)
                split_ahead(db + 2, groups)
                split_ahead(db + 3, groups)

                def keys_out(n):
                    c = 9 * l + n
                    for s in (1, 3):
                        dve.wait_ge(at_tr, 4 * c + s + 1)
                        if n >= 2:
                            dve.wait_ge(at_sc, c - 1)
                        nc.vector.tensor_copy(st_att["kt"][:, c % 2, 2 * s:2 * s + 2, :], ps[:, 1, :].rearrange("p (b m) -> p b m", b=2)).then_inc(at_kv, 1)

                def row_max(t, rows, banks):
                    s = ps[0:rows, banks:banks + 2, :].rearrange("p a (b m) -> p (a b) m", b=2)
                    link(nc.vector.tensor_reduce(st_att["rs"][0:rows, t, :], s, AX_X, ALU.max))
                    nc.vector.tensor_scalar(st_att["mx"][0:rows, t, :], st_att["rs"][0:rows, t, :], -float(D // XH) ** -0.5, None, ALU.mult).then_inc(at_max, 1)

                def normalise(t, rows):
                    dve.wait_ge(at_exp, 3 * l + t + 1)
                    link(nc.vector.reciprocal(st_att["rs"][0:rows, t, :], st_att["sum"][0:rows, t, :]))
                    pp = st_att["p"][0:rows, t % 2]
                    nc.vector.tensor_tensor(pp, pp, st_att["rs"][0:rows, t, :].unsqueeze(2).to_broadcast([rows, XH, MEM]), ALU.mult).then_inc(at_p, 1)

                keys_out(0)
                dve.wait_ge(at_sc, 9 * l + 1)
                row_max(0, P, 4)
                row_max(1, P, 6)
                normalise(0, P)
                normalise(1, P)
                for n in range(1, 9):
                    keys_out(n)
                dve.wait_ge(at_sn, l + 1)
                row_max(2, 64, 0)
                dve.wait_ge(at_oh, 2 * l + 1)
                nc.vector.tensor_tensor(xt_lo[:, :, 0:PROMPT], ps[:, 4:8, :].rearrange("p a (b q) -> p (a b) q", b=2),
                                        xt_hi[:, :, 0:PROMPT].bitcast(F32), ALU.subtract).then_inc(at_ol, 1)
                normalise(2, 64)
                dve.wait_ge(at_oh, 2 * l + 2)
                nc.vector.tensor_tensor(xt_lo[:, :, PROMPT:NT], ps[:, 2, :].rearrange("p (b q) -> p b q", b=8),
                                        xt_hi[:, :, PROMPT:NT].bitcast(F32), ALU.subtract).then_inc(at_ol, 1)
                add_block(db + 4, groups, 0)
                add_block(db + 5, groups, 1)
                layer_norm(3 * l + 1)
                transposed(3 + 3 * l, TILES)
                m, s = st_moe, mo[l]
                dve.wait_ge(s["xh"], 1)
                link(nc.vector.tensor_tensor(m["xn_lo"][:], x[:], m["xn_hi"][:].bitcast(F32), ALU.subtract))
                link(nc.vector.tensor_scalar(x[:], x[:], ALPHA, None, ALU.mult))
                dve.wait_ge(rt_e, l + 1)
                inverse(m["sc"][:])
                V_ = nc.vector
                link(V_.tensor_tensor(m["sel"][:], m["sc"][:], r_bias[:].unsqueeze(1).to_broadcast([P, TILES, EXPERTS]), ALU.add))
                for t in range(TILES):
                    sel = m["sel"][:, t, :].rearrange("p (g e) -> p g e", g=GROUPS)
                    V_.tensor_tensor(m["pair"][:, t, :, 0:3], sel[:, :, 0:3], sel[:, :, 1:4], ALU.add)
                    V_.tensor_tensor(m["pair"][:, t, :, 3:5], sel[:, :, 0:2], sel[:, :, 2:4], ALU.add)
                    ins = V_.tensor_tensor(m["pair"][:, t, :, 5:6], sel[:, :, 0:1], sel[:, :, 3:4], ALU.add)
                link(ins)
                link(V_.tensor_reduce(m["gs"][:], m["pair"][:], AX_X, ALU.max))
                link(V_.tensor_reduce(m["gm"][:], m["gs"][:], AX_X, ALU.max))

                def first_of(out, values, best, rank, n):
                    link(V_.tensor_tensor(out, values, best.unsqueeze(2).to_broadcast([P, TILES, n]), ALU.is_equal))
                    link(V_.tensor_tensor(out, out, rank.unsqueeze(1).to_broadcast([P, TILES, n]), ALU.mult))
                    link(V_.tensor_reduce(m["m1"][:], out, AX_X, ALU.max))
                    link(V_.tensor_tensor(out, out, m["m1"][:].unsqueeze(2).to_broadcast([P, TILES, n]), ALU.is_equal))

                first_of(m["g"][:], m["gs"][:], m["gm"][:], e_rank[:, 0:GROUPS], GROUPS)
                link(V_.memset(m["g"][64:P, 2, :], 0.0))
                V_.engine_nop().then_inc(rt_g, 1)
                gb = m["g"][:].unsqueeze(3).to_broadcast([P, TILES, GROUPS, EPG])
                for t in range(TILES):
                    ins = V_.tensor_copy(m["r1"][:, t, :].rearrange("p (g e) -> p g e", g=GROUPS), m["g"][:, t, :].unsqueeze(2).to_broadcast([P, GROUPS, EPG]))
                link(ins)
                link(V_.tensor_tensor(m["sel"][:], m["sel"][:], m["r1"][:], ALU.mult))
                link(V_.tensor_scalar(m["r1"][:], m["r1"][:], BIG, -BIG, ALU.mult, ALU.add))
                link(V_.tensor_tensor(m["sel"][:], m["sel"][:], m["r1"][:], ALU.add))
                link(V_.tensor_reduce(m["gm"][:], m["sel"][:], AX_X, ALU.max))
                first_of(m["r2"][:], m["sel"][:], m["gm"][:], e_rank[:], EXPERTS)
                link(V_.tensor_scalar(m["r1"][:], m["r2"][:], -2 * BIG, None, ALU.mult))
                link(V_.tensor_tensor(m["sel"][:], m["sel"][:], m["r1"][:], ALU.add))
                link(V_.tensor_reduce(m["gm"][:], m["sel"][:], AX_X, ALU.max))
                first_of(m["r3"][:], m["sel"][:], m["gm"][:], e_rank[:], EXPERTS)
                link(V_.tensor_tensor(m["r2"][:], m["r2"][:], m["r3"][:], ALU.add))
                link(V_.tensor_tensor(m["r2"][:], m["r2"][:], m["sc"][:], ALU.mult))
                link(V_.tensor_reduce(m["gm"][:], m["r2"][:], AX_X, ALU.add))
                link(V_.reciprocal(m["gm"][:], m["gm"][:]))
                link(V_.tensor_tensor(m["r2"][:], m["r2"][:], m["gm"][:].unsqueeze(2).to_broadcast([P, TILES, EXPERTS]), ALU.mult))
                for t in range(TILES):
                    ins = V_.tensor_reduce(comb4[:, t, :], m["r2"][:, t, :].rearrange("p (g e) -> p e g", g=GROUPS), AX_X, ALU.add)
                link(ins)
                dve.wait_ge(rt_pos, l + 1)
                link(V_.tensor_copy(m["pos"][:].rearrange("p t g -> p (t g)"), ps[:, 5, 0:TILES * GROUPS]))
                link(V_.tensor_scalar(m["p2"][:], m["pos"][:], 128.0, 384.0, ALU.is_ge, ALU.mult))
                link(V_.tensor_tensor(m["p2"][:], m["pos"][:], m["p2"][:], ALU.add))
                link(V_.tensor_scalar(m["pos"][:], m["pos"][:], 256.0, 384.0, ALU.is_ge, ALU.mult))
                link(V_.tensor_tensor(m["p2"][:], m["p2"][:], m["pos"][:], ALU.add))
                link(V_.tensor_tensor(m["p2"][:], m["p2"][:], g_base[:].unsqueeze(1).to_broadcast([P, TILES, GROUPS]), ALU.add))
                link(V_.tensor_tensor(m["p2"][:], m["p2"][:], m["g"][:], ALU.mult))
                link(V_.tensor_reduce(u_slot[:], m["p2"][:], AX_X, ALU.add))
                V_.tensor_scalar(u_slot[:], u_slot[:], -1.0, None, ALU.add).then_inc(s["add"], 1)
                link(V_.tensor_reduce(m["mc"][:], ps[:, 5, TILES * GROUPS:TILES * GROUPS + GROUPS], AX_X, ALU.max))
                link(V_.tensor_scalar(m["mc2"][:], m["mc"][:], 128.0, 4.0, ALU.is_gt, ALU.mult))
                link(V_.tensor_scalar(m["mc"][:], m["mc"][:], 256.0, 4.0, ALU.is_gt, ALU.mult))
                link(V_.tensor_tensor(m["mc"][:], m["mc"][:], m["mc2"][:], ALU.add))
                link(V_.tensor_scalar(m["mc"][:], m["mc"][:], 4.0, None, ALU.add))
                V_.tensor_copy(n_iter[:], m["mc"][0:1, :]).then_inc(rt_n, 1)
                V_.engine_nop().then_inc(s["h"], 1)
                dve.wait_ge(rt_n, l + 1)
                n = dve.value_load(n_iter[0:1, 0:1], min_val=4, max_val=12)
                base = splits[0]
                with dve.Fori(0, n) as i:
                    g = i if groups is None else groups + i
                    dve.wait_ge(s["add"], i * 6 + 1)
                    for t in range(TILES):
                        ins = V_.tensor_scalar(m["pick"][:, t, :], slot_no[:], u_slot[:, t:t + 1], None, ALU.is_equal)
                    ins.then_inc(s["p"], 1)
                    for j in range(3):
                        split(base + j, g)
                    dve.wait_ge(s["p"], i + 1)
                    V_.tensor_scalar(u_slot[:], u_slot[:], -float(P), None, ALU.add).then_inc(s["step"], 1)
                    dve.wait_ge(s["xgh"], i + 1)
                    V_.tensor_tensor(m["xg_lo"][:].rearrange("p (a k) s -> p a (k s)", a=2), ps[:, 4:6, :],
                                     m["xg_hi"][:].rearrange("p (a k) s -> p a (k s)", a=2).bitcast(F32), ALU.subtract).then_inc(s["xgl"], 1)
                    for j in range(3, GCH):
                        split(base + j, g)
                        for e in range(EPG):
                            if j == GU_LAST[e] + 3:
                                dve.wait_ge(s["sil"], i * EPG + e + 1)
                                V_.scalar_tensor_tensor(out=m["h"][:, e % 2, :], in0=m["sil"][:], scalar=m["cw"][:, e:e + 1],
                                                        in1=ps[:, 2 * (e % 2) + 1, :], op0=ALU.mult, op1=ALU.mult).then_inc(s["h"], 1)
                        if j - 3 in T_AFTER:
                            e = T_AFTER[j - 3]
                            dve.wait_ge(s["hth"], i * EPG + e + 1)
                            V_.tensor_tensor(m["ht_lo"][:, e % 2], ps[:, 6, :].rearrange("p (k s) -> p k s", k=4),
                                             m["ht_hi"][:, e % 2].bitcast(F32), ALU.subtract).then_inc(s["htl"], 1)
                    dve.wait_ge(s["step"], i + 1)
                    dve.wait_ge(s["yh"], i + 1)
                    V_.tensor_tensor(m["y_lo"][:].rearrange("p (a c) -> p a c", a=2), ps[:, 4:6, :],
                                     m["y_hi"][:].rearrange("p (a c) -> p a c", a=2).bitcast(F32), ALU.subtract).then_inc(s["yl"], 1)
                    for r, bank in enumerate((0, 1, 2, 3, 6, 7)):
                        dve.wait_ge(s["s"], i * 6 + r + 1)
                        cols = x[:, r // 2, (r % 2) * NB:(r % 2 + 1) * NB]
                        V_.tensor_tensor(cols, cols, ps[:, bank, :], ALU.add).then_inc(s["add"], 1)
                groups = n
                dve.wait_ge(s["add"], n * 6 + 1)
                layer_norm(3 * l + 2)
                if l == 0:
                    transposed(4, TILES)

        @block.tensor
        def _(pe):
            mm = nc.tensor.matmul

            def three(out, hi_w, lo_w, hi_x, lo_x, start, stop, x_moves):
                for n, (w, v) in enumerate(((hi_w, hi_x), (hi_w, lo_x), (lo_w, hi_x)) if x_moves else
                                           ((hi_w, hi_x), (lo_w, hi_x), (hi_w, lo_x))):
                    lhs, rhs = (w, v) if x_moves else (v, w)
                    ins = mm(out, lhs, rhs, start=start and n == 0, stop=stop and n == 2)
                return ins

            def dense(db, groups, mode, tiles=TILES):
                par = db % 2
                if db >= 2:
                    pe.wait_ge(evac[par], db // 2)
                for half in range(2):
                    k = 2 * db + half
                    r = k % RING
                    pe.wait_ge(w_low, at(k + 1, groups, GCH))
                    for kc in range(4):
                        kt = 4 * half + kc
                        start, stop = kt == 0, kt == KT - 1
                        if mode == "T":
                            for n in range(4):
                                cols = slice(n * P, (n + 1) * P)
                                ins = three(ps[:, 4 * par + n, 0:NT], w_hi[:, r, kc, cols], w_lo[:, r, kc, cols],
                                            xt_hi[:, kt, 0:NT], xt_lo[:, kt, 0:NT], start, stop, True)
                        else:
                            for t in range(tiles):
                                toks = slice(t * P, (t + 1) * P)
                                ins = three(ps[:, 4 * par + t, :], w_hi[:, r, kc, :], w_lo[:, r, kc, :],
                                            xt_hi[:, kt, toks], xt_lo[:, kt, toks], start, stop, False)
                    ins.then_inc(w_used, 1)

            def transpose_in(u, src, tiles):
                for kt in range(KT):
                    if kt >= 4:
                        pe.wait_ge(xt_l, 8 * u + kt - 3)
                    for t in range(tiles):
                        ins = nc.tensor.transpose(ps[:, kt % 4, t * P:(t + 1) * P], src[:, t, kt * P:(kt + 1) * P], ident[:])
                    ins.then_inc(xt_ps, 1)
                pe.wait_ge(xt_l, 8 * u + 8)

            def head_scores(l, h):
                m, n = st_mix[l], l * 8 + h
                e = m["e"][:, h % 2]
                pe.wait_ge(hd_m, n + 1)
                if h:
                    pe.wait_ge(hd_msk, n)
                for t in range(TILES):
                    w = P if t < 2 else 64
                    toks = slice(t * P, t * P + w)
                    ins = mm(ps[0:w, 0, t * P:t * P + w], e[:, 1, toks], e[:, 0, toks], start=True, stop=True)
                ins.then_inc(hd_sc, 1)
                for t in range(TILES):
                    w = P if t < 2 else 64
                    ins = nc.tensor.transpose(ps[0:w, 1, t * P:(t + 1) * P], e[:, 3, t * P:t * P + w], ident[:])
                ins.then_inc(hd_tr, 1)

            def head(l, h):
                H, V, VB, _ = mixer_shape(l)
                m, n = st_mix[l], l * 8 + h
                e = m["e"][:, h % 2]
                vcols = slice(h * V, (h + 1) * V)

                def updates(pair):
                    t, row, bank = pair // 4, 32 * (pair % 4), 2 + pair % 4
                    if pair >= 4:
                        pe.wait_ge(hd_s, NCH * n + 2 * (pair - 4) + 2)
                    for c in range(2):
                        ins = mm(ps[:, bank, c * V:(c + 1) * V], m["kn"][row:row + 32, t, c, :], m["v"][row:row + 32, t, vcols],
                                 start=True, stop=True)
                    ins.then_inc(hd_u, 1)

                def read_state(c):
                    pe.wait_ge(hd_s, NCH * n + c)
                    for vb in range(VB):
                        ins = mm(ps[:, 6 + vb, c * CH:(c + 1) * CH], m["s"][:, (c - 1) % 8, vb * P:(vb + 1) * P],
                                 e[:, 2, c * CH:(c + 1) * CH], start=False, stop=True, skip_group_check=True)
                    ins.then_inc(hd_i, 1)

                pe.wait_ge(hd_kn, n + 1)
                if h:
                    pe.wait_ge(hd_ss, SAMPLES * n)
                for pair in range(4):
                    updates(pair)
                pe.wait_ge(hd_msk, n + 1)
                if h:
                    pe.wait_ge(hd_y, n)
                for vb in range(VB):
                    vc = slice(h * V + vb * P, h * V + (vb + 1) * P)
                    for t in range(TILES):
                        w = P if t < 2 else 64
                        mm(ps[:, 6 + vb, t * P:t * P + w], m["v"][0:w, t, vc], m["sc"][0:w, t, 0:w],
                           start=t == 0, stop=True, skip_group_check=True)
                for c in range(1, NCH):
                    read_state(c)
                    if c % 2 == 0 and c // 2 + 3 < NCH // 2:
                        updates(c // 2 + 3)
                pe.wait_ge(s0_in, 16 * (n + 1))
                pe.wait_ge(hd_s, NCH * (n + 1))
                for bb in range(SAMPLES):
                    toks = slice(PROMPT + 8 * bb, PROMPT + 8 * bb + 8)
                    for vb in range(VB):
                        mm(ps[:, 6 + vb, toks], m["s0"][:, bb, vb * P:(vb + 1) * P], e[:, 2, toks],
                           start=False, stop=True, skip_group_check=True)
                    row = 32 * (bb // 4)
                    ins = mm(ps[:, 2 + bb // 2, (bb % 2) * V:(bb % 2 + 1) * V], m["ks"][row:row + 32, bb % 4, :],
                             m["v"][row:row + 32, 2, vcols], start=True, stop=True)
                    if bb % 2:
                        ins.then_inc(hd_su, 1)
                mm(ps[:, 6 + VB - 1, 504:506], ident[:], ones[:, 0:2], start=False, stop=True, skip_group_check=True).then_inc(hd_o, 1)

            def head_mean(l, h):
                H, V, VB, _ = mixer_shape(l)
                m, n = st_mix[l], l * 8 + h
                pe.wait_ge(hd_sq, n + 1)
                for vb in range(VB):
                    ins = mm(ps[:, 1, 0:NT], ones[:], m["sq"][:, vb, :], start=vb == 0, stop=vb == VB - 1)
                ins.then_inc(hd_ms, 1)

            pe.wait_ge(consts, 1)
            pe.wait_ge(consts_in, 160)
            pe.wait_ge(mem_in, 16)
            transpose_in(0, st_kv["mem"], 2)
            for db in range(KV_BLOCKS):
                dense(db, None, "N", 2)
            pe.wait_ge(x_in, 32)
            pe.wait_ge(x_pad, 1)
            for par in range(2):
                pe.wait_ge(evac[par], KV_BLOCKS // 2)
            transpose_in(1, x, TILES)
            groups = None
            for l in range(LAYERS):
                H, V, VB, _ = mixer_shape(l)
                for nb in range(IN_BLOCKS[l]):
                    kind, c = block_kind(l, nb)
                    dense(first_block(l) + nb, groups, "N" if kind == "v" else "T")
                    if l == 1 and kind == "k":
                        pe.wait_ge(evac[0], (first_block(l) + nb - 1) // 2 + 1)
                        for kt in range(KT):
                            for r, xx in enumerate((xt_hi, xt_lo)):
                                ins = mm(ps[0:16, 3, 0:NT], w_lr[:, kt, :], xx[:, kt, 0:NT].bitcast(F32),
                                         start=kt == 0 and r == 0, stop=kt == KT - 1 and r == 1)
                        ins.then_inc(mx_lr, 1)
                        pe.wait_ge(mx_lrc, 1)
                        for hh in range(4):
                            if hh >= 2:
                                pe.wait_ge(mx_inv, 4 + hh - 1)
                            mm(ps[:, hh % 2, 0:NT], w_gk[:, hh * P:(hh + 1) * P], lr_t[:], start=True, stop=True).then_inc(mx_z, 1)
                        pe.wait_ge(mx_inv, 4 + 4)
                last = first_block(l) + IN_BLOCKS[l]
                for d in (last - 2, last - 1):
                    pe.wait_ge(evac[d % 2], d // 2 + 1)
                for h in range(H):
                    head_scores(l, h)
                    head(l, h)
                    head_mean(l, h)
                    pe.wait_ge(hd_ms, 2 * (l * 8 + h + 1))
                pe.wait_ge(hd_fin, l * 8 + H)
                db = last
                dense(db, groups, "N")
                dense(db + 1, groups, "N")
                pe.wait_ge(ln_done, TILES * (3 * l + 1))
                transpose_in(2 + 3 * l, x, TILES)
                dense(db + 2, groups, "T")
                dense(db + 3, groups, "T")
                for d in (db + 2, db + 3):
                    pe.wait_ge(evac[d % 2], d // 2 + 1)
                t_ = st_att

                def keys_in(n):
                    c = 9 * l + n
                    par = c % 2
                    pe.wait_ge(k_in[par], 16 * (c // 2 + 1))
                    for s in range(4):
                        if s >= 2:
                            pe.wait_ge(at_ka if s == 2 else at_kv, 2 * c + 1)
                        elif n:
                            pe.wait_ge(at_ka if s == 0 else at_kv, 2 * c)
                        for b2 in range(2):
                            for mh in range(2):
                                ins = nc.tensor.transpose(ps[:, s % 2, b2 * MEM + mh * P:b2 * MEM + (mh + 1) * P],
                                                          t_["kn"][:, par, mh, (2 * s + b2) * P:(2 * s + b2 + 1) * P], ident[:])
                        ins.then_inc(at_tr, 1)
                    pe.wait_ge(at_ka, 2 * c + 2)
                    pe.wait_ge(at_kv, 2 * c + 2)

                keys_in(0)
                for t in range(2):
                    for hh in range(XH):
                        for kc in range(2):
                            ins = mm(ps[:, 4 + 2 * t + hh // 2, (hh % 2) * MEM:(hh % 2 + 1) * MEM], t_["q"][:, 2 * hh + kc, t * P:(t + 1) * P],
                                     t_["kt"][:, (9 * l) % 2, 2 * hh + kc, :], start=kc == 0, stop=kc == 1)
                ins.then_inc(at_sc, 1)
                for n in range(1, 9):
                    keys_in(n)
                    toks = slice(PROMPT + 8 * (n - 1), PROMPT + 8 * n)
                    for hh in range(XH):
                        for mh in range(2):
                            off = (mh * XH + hh) * 64 + 8 * (n - 1)
                            for kc in range(2):
                                ins = mm(ps[:, 2, off:off + 8], t_["kt"][:, (9 * l + n) % 2, 2 * hh + kc, mh * P:(mh + 1) * P],
                                         t_["q"][:, 2 * hh + kc, toks], start=kc == 0, stop=kc == 1)
                    ins.then_inc(at_sc, 1)
                mm(ps[:, 3, 0:2], ident[:], ones[:, 0:2], start=True, stop=True).then_inc(at_st, 1)
                pe.wait_ge(at_sts, l + 1)
                for hh in range(XH):
                    for mh in range(2):
                        ins = nc.tensor.transpose(ps[0:64, hh // 2, (hh % 2) * MEM + mh * P:(hh % 2) * MEM + (mh + 1) * P],
                                                  t_["sts"][:, mh, hh, :], ident[:])
                ins.then_inc(at_sn, 1)
                for r in range(4):
                    if r % 2 == 0:
                        pe.wait_ge(at_p, 3 * l + r // 2 + 1)
                    if r >= 2:
                        pe.wait_ge(at_pte, 5 * l + r - 1)
                    for hh in range(XH):
                        ins = nc.tensor.transpose(ps[:, 3 if r % 2 else 2, hh * P:(hh + 1) * P],
                                                  t_["p"][:, r // 2, hh, (r % 2) * P:(r % 2 + 1) * P], ident[:])
                    ins.then_inc(at_pt, 1)
                pe.wait_ge(at_pte, 5 * l + 4)
                c = 9 * l
                pe.wait_ge(v_in[c % 2], 16 * (c // 2 + 1))
                for b8 in range(8):
                    for mh in range(2):
                        ins = mm(ps[:, 4 + b8 // 2, (b8 % 2) * PROMPT:(b8 % 2 + 1) * PROMPT], t_["vn"][:, c % 2, mh, b8 * P:(b8 + 1) * P],
                                 t_["pt"][:, mh, b8 // 2, :], start=mh == 0, stop=mh == 1)
                ins.then_inc(at_pv, 1)
                pe.wait_ge(at_p, 3 * l + 3)
                for hh in range(XH):
                    for mh in range(2):
                        ins = nc.tensor.transpose(ps[:, 3, (mh * XH + hh) * 64:(mh * XH + hh + 1) * 64],
                                                  t_["p"][0:64, 0, hh, mh * P:(mh + 1) * P], ident[0:64, 0:64])
                ins.then_inc(at_pt, 1)
                pe.wait_ge(at_pte, 5 * l + 5)
                for n in range(1, 9):
                    c = 9 * l + n
                    pe.wait_ge(v_in[c % 2], 16 * (c // 2 + 1))
                    for b8 in range(8):
                        off = b8 * 64 + 8 * (n - 1)
                        for mh in range(2):
                            ins = mm(ps[:, 2, off:off + 8], t_["vn"][:, c % 2, mh, b8 * P:(b8 + 1) * P],
                                     t_["pts"][:, mh, b8 // 2, 8 * (n - 1):8 * n], start=mh == 0, stop=mh == 1)
                    ins.then_inc(at_pv, 1)
                pe.wait_ge(at_ol, 2 * l + 2)
                dense(db + 4, groups, "N")
                dense(db + 5, groups, "N")
                pe.wait_ge(ln_done, TILES * (3 * l + 2))
                transpose_in(3 + 3 * l, x, TILES)
                for t in range(TILES):
                    for kt in range(KT):
                        for r, xx in enumerate((xt_hi, xt_lo)):
                            ins = mm(ps[:, 4, t * EXPERTS:(t + 1) * EXPERTS], xx[:, kt, t * P:(t + 1) * P].bitcast(F32), router[:, kt, :],
                                     start=kt == 0 and r == 0, stop=kt == KT - 1 and r == 1)
                ins.then_inc(rt_ps, 1)
                m, s = st_moe, mo[l]
                pe.wait_ge(rt_g, l + 1)
                for t in range(TILES):
                    for t2 in range(t + 1):
                        mm(ps[:, 5, t * GROUPS:(t + 1) * GROUPS], (before if t2 == t else ones)[:], m["g"][:, t2, :], start=t2 == 0, stop=t2 == t)
                for t in range(TILES):
                    ins = mm(ps[:, 5, TILES * GROUPS:(TILES + 1) * GROUPS], ones[:], m["g"][:, t, :], start=t == 0, stop=t == TILES - 1)
                ins.then_inc(rt_pos, 1)
                pe.wait_ge(rt_n, l + 1)
                n = pe.value_load(n_iter[0:1, 0:1], min_val=4, max_val=12)
                base = 2 * (BLOCKS0 if l == 0 else BLOCKS1)
                with pe.Fori(0, n) as i:
                    g = i if groups is None else groups + i
                    pe.wait_ge(s["add"], i * 6 + 1)
                    pe.wait_ge(s["p"], i + 1)
                    for kt in range(KT):
                        for t in range(TILES):
                            for r, xx in enumerate((m["xn_hi"], m["xn_lo"])):
                                ins = mm(ps[:, 4 + kt // 4, (kt % 4) * P:(kt % 4 + 1) * P], xx[:, t, kt * P:(kt + 1) * P], m["pick"][:, t, :],
                                         start=t == 0 and r == 0, stop=t == TILES - 1 and r == 1)
                    ins.then_inc(s["g"], 1)
                    for t in range(TILES):
                        nc.tensor.transpose(ps[:, 7, t * P:(t + 1) * P], m["pick"][:, t, :].bitcast(F32), ident[:])
                    for t in range(TILES):
                        ins = mm(ps[:, 7, TILES * P:TILES * P + EPG], m["pick"][:, t, :].bitcast(F32), comb4[:, t, :], start=t == 0, stop=t == TILES - 1)
                    ins.then_inc(s["pt"], 1)
                    pe.wait_ge(s["xgl"], i + 1)
                    for j, (what, e, half) in enumerate(MOE_ORDER):
                        k = base + j
                        r = k % RING
                        if what == "gate" and half == 0 and e >= 2:
                            pe.wait_ge(s["h"], i * EPG + e)
                        if what == "down" and half == 0:
                            pe.wait_ge(s["htl"], i * EPG + e + 1)
                        pe.wait_ge(w_low, at(k + 1, g, GCH))
                        for kc in range(4):
                            if what == "down":
                                ins = three(ps[:, 4 + half, :], w_hi[:, r, kc, :], w_lo[:, r, kc, :], m["ht_hi"][:, e % 2, kc, :],
                                            m["ht_lo"][:, e % 2, kc, :], e == 0 and kc == 0, e == EPG - 1 and kc == 3, False)
                            else:
                                kt = 4 * half + kc
                                ins = three(ps[:, 2 * (e % 2) + (what == "up"), :], w_hi[:, r, kc, :], w_lo[:, r, kc, :], m["xg_hi"][:, kt, :],
                                            m["xg_lo"][:, kt, :], kt == 0, kt == KT - 1, False)
                        ins.then_inc(w_used, 1)
                        if j in T_AFTER:
                            e2 = T_AFTER[j]
                            pe.wait_ge(s["h"], i * EPG + e2 + 2)
                            if e2:
                                pe.wait_ge(s["htl"], i * EPG + e2)
                            for kc in range(4):
                                ins = nc.tensor.transpose(ps[:, 6, kc * P:(kc + 1) * P], m["h"][:, e2 % 2, kc * P:(kc + 1) * P], ident[:])
                            ins.then_inc(s["t"], 1)
                    pe.wait_ge(s["yl"], i + 1)
                    for r, bank in enumerate((0, 1, 2, 3, 6, 7)):
                        cols = slice((r % 2) * NB, (r % 2 + 1) * NB)
                        mm(ps[:, bank, :], m["pick_t"][:, (r // 2) * P:(r // 2 + 1) * P], m["y_hi"][:, cols], start=True, stop=False)
                        mm(ps[:, bank, :], m["pick_t"][:, (r // 2) * P:(r // 2 + 1) * P], m["y_lo"][:, cols], start=False, stop=True).then_inc(s["s"], 1)
                groups = n
                if l == 0:
                    pe.wait_ge(ln_done, TILES * 3)
                    transpose_in(4, x, TILES)


_INS = ["x_prompt", "x_sample", "state_hgrn", "state_gla", "cache_mem_k", "cache_mem_v", "mem_prompt",
        "hgrn_w_in", "hgrn_lb_logits", "hgrn_norm_g", "hgrn_w_out", "gla_w_in", "gla_w_gk2", "gla_b_gk2",
        "gla_norm_g", "gla_w_out", "xattn_w_q", "xattn_w_kv", "xattn_w_o", "router_w", "router_bias",
        "moe_w_gate", "moe_w_up", "moe_w_down", "ln_g", "ln_b"]
_OUTS = [("y_prompt", (1, PROMPT, D)), ("y_sample", (SAMPLES, SAMPLE_T, D)),
         ("state_hgrn_prompt", (1, 1, 8, 128, 128)), ("state_gla_prompt", (1, 1, 4, 128, 256)),
         ("mem_k_prompt", (2, 1, MEM, XH, 256)), ("mem_v_prompt", (2, 1, MEM, XH, 256)),
         ("state_hgrn_sample", (1, 8, 8, 128, 128)), ("state_gla_sample", (1, 8, 4, 128, 256))]


def kernel(**inputs):
    import numpy as _np
    import concourse.bacc as _bacc
    from concourse.bass_utils import run_bass_kernel_spmd as _run

    nc = _bacc.Bacc("TRN2", target_bir_lowering=False, num_devices=1)
    arrays, aps = {}, {}
    for name in _INS:
        arrays[f"in_{name}"] = _np.ascontiguousarray(inputs[name])
        aps[name] = nc.dram_tensor(f"in_{name}", arrays[f"in_{name}"].shape, F32, kind="ExternalInput").ap()
    for name, shape in _OUTS:
        aps[name] = nc.dram_tensor(f"out_{name}", shape, F32, kind="ExternalOutput").ap()
    decoder_step(nc, aps)
    r = _run(nc, [arrays], core_ids=[0])
    return tuple(r.results[0][f"out_{name}"] for name, _ in _OUTS)
```

```python
from contextlib import ExitStack

import concourse.bass as bass
from concourse import mybir

F32 = mybir.dt.float32
F32R = mybir.dt.float32r
I32 = mybir.dt.int32
U32 = mybir.dt.uint32
ACT = mybir.ActivationFunctionType
ALU = mybir.AluOpType
AX_X = mybir.AxisListType.X

P = 128
D = 1024
KT = D // P
LAYERS = 2
PROMPT = 256
SAMPLES, SAMPLE_T = 8, 8
NT = PROMPT + SAMPLES * SAMPLE_T
TILES = 3
CH = 16
NCH = PROMPT // CH
MEM = 256
XH = 4
EXPERTS, GROUPS, EPG = 16, 4, 4
F = 512
ALPHA = (2 * LAYERS) ** 0.25
LN_EPS, RMS_EPS = 1e-5, 1e-6
GATE_NORM = 16.0
BIG = 1e30
RING = 3
NB = 512
GCH = 24
KV_BLOCKS = 2 * 4
IN_BLOCKS = (8, 6)
BLOCKS0 = KV_BLOCKS + IN_BLOCKS[0] + 6
BLOCKS1 = BLOCKS0 + IN_BLOCKS[1] + 6

MOE_ORDER = []
for _e in range(EPG):
    MOE_ORDER += [("gate", _e, 0), ("gate", _e, 1), ("up", _e, 0), ("up", _e, 1)]
    if _e:
        MOE_ORDER += [("down", _e - 1, 0), ("down", _e - 1, 1)]
MOE_ORDER += [("down", EPG - 1, 0), ("down", EPG - 1, 1)]
GU_LAST = [MOE_ORDER.index(("up", e, 1)) for e in range(EPG)]
T_AFTER = {GU_LAST[1] - 2: 0, GU_LAST[1] + 4: 1, GU_LAST[2] + 4: 2, GU_LAST[3] + 1: 3}
MRING = 4
SIDE = {1: ("s", 0), 3: ("s", 1), 5: ("s", 2), 7: ("s", 3), 9: ("s", 4), 11: ("s", 5),
        12: ("pt", 0), 14: ("g", 0), 16: ("g", 1), 20: ("t", 0), 21: ("t", 1)}


def mixer_shape(l):
    return (8, 128, 1, 1.0) if l == 0 else (4, 256, 2, 1.0 / GATE_NORM)


def first_block(l):
    return KV_BLOCKS if l == 0 else BLOCKS0


def block_kind(l, n):
    kinds = [("f", 2), ("q", 2), ("gate", 2), ("v", 2)] if l == 0 else [("q", 1), ("k", 1), ("gate", 2), ("v", 2)]
    for kind, count in kinds:
        if n < count:
            return kind, n
        n -= count


BATCHES = 1 + SAMPLES
KV_CHUNKS = 2 * BATCHES
CHUNKS0 = 2 * BLOCKS0 + KV_CHUNKS
CHUNKS1 = 2 * BLOCKS1 + 2 * KV_CHUNKS


def chunk_no(db):
    k = 2 * db
    for l in range(LAYERS):
        if db >= first_block(l) + IN_BLOCKS[l] + 4:
            k += KV_CHUNKS
    return k


def keys_no(l):
    return chunk_no(first_block(l) + IN_BLOCKS[l] + 3) + 2


def in_end(l):
    return chunk_no(first_block(l) + IN_BLOCKS[l])


def fills(l, h, samples):
    per = [(SAMPLES if samples else NCH) * mixer_shape(x)[1] // NB for x in range(LAYERS)]
    return per[l] * h + (per[0] * mixer_shape(0)[0] if l else 0)


def split_limit(db):
    ends = sorted([in_end(0), keys_no(0), CHUNKS0, in_end(1), keys_no(1), CHUNKS1])
    return next(end for end in ends if chunk_no(max(db, 0)) < end)


def slot_of(k):
    return (k if k < CHUNKS0 else k - CHUNKS0) % RING


def loads_of(k):
    if k < CHUNKS0:
        return k // RING + 1
    r, k = slot_of(k), k - CHUNKS0
    return len(range(r, CHUNKS0, RING)) + k // RING + 1


def moe_loads_of(l, j):
    r = j % MRING
    dense = [0, CHUNKS0] if l == 0 else [0, CHUNKS0, CHUNKS1]
    before = sum(len(range(r, b - a, RING)) for a, b in zip(dense, dense[1:])) if r < RING else 0
    return before + j // MRING + 1


SKIPPED = 6


def side_start(i):
    return SKIPPED + 4 if isinstance(i, int) and i == 0 else i * 12 + 4


def key_copies(l, n, s):
    return 34 * l + (s // 2 + 1 if n == 0 else 4 * n - 1 + s)


def side_order(first, last):
    out = [(-1, "cw", 0)]
    for j, (what, n) in sorted(SIDE.items()):
        if (what == "s" and first) or (what in "gt" and last):
            continue
        out.append((j, what, n))
    return out


def at(static, groups, per):
    return static if groups is None else groups * per + static


def decoder_step(nc, a):
    with ExitStack() as ctx:
        def sb(name, shape, dt=F32):
            return ctx.enter_context(nc.sbuf_tensor(name, shape, dt))

        def sem(name):
            return ctx.enter_context(nc.semaphore(name))

        raw = sb("raw", [P, RING, 4, NB])
        w_hi = sb("w_hi", [P, RING, 4, NB], F32R)
        w_lo = sb("w_lo", [P, RING, 4, NB], F32R)
        x = sb("x", [P, TILES, D])
        xt_hi = sb("xt_hi", [P, KT, TILES * P], F32R)
        xt_lo = sb("xt_lo", [P, KT, TILES * P], F32R)
        ln_gb = sb("ln_gb", [P, 2, D])
        ident = sb("ident", [P, P])
        ones = sb("ones", [P, P])
        eps = sb("eps", [P, 1])
        before = sb("before", [P, P])
        slot_no = sb("slot_no", [P, P])
        mask16 = sb("mask16", [P, P], U32)
        mask8 = sb("mask8", [P, 64], U32)
        batch_of = sb("batch_of", [32, P])
        mask_f = sb("mask_f", [P, P])
        carry = sb("carry", [P, NT])
        lb_rows = sb("lb_rows", [P, 3, 8])
        lb = sb("lb", [P, 8])
        one_m_lb = sb("one_m_lb", [P, 8])
        lb_tmp = sb("lb_tmp", [P, 8])
        gain_a = sb("gain_a", [P, 1])
        gain_b = sb("gain_b", [P, 2])
        b_gk = sb("b_gk", [P, 4])
        w_gk = sb("w_gk", [16, 512])
        w_lr = sb("w_lr", [P, KT, 16])
        lr_t = sb("lr_t", [16, NT])
        router = sb("router", [P, KT, EXPERTS])
        r_hi = sb("r_hi", [P, KT, EXPERTS], F32R)
        r_lo = sb("r_lo", [P, KT, EXPERTS], F32R)
        r_bias = sb("r_bias", [P, EXPERTS])
        g_base = sb("g_base", [P, GROUPS])
        e_rank = sb("e_rank", [P, EXPERTS])
        stats = sb("stats", [P, TILES, 12])
        mean_var = sb("mean_var", [P, TILES, 2])
        rstd = sb("rstd", [P, TILES])
        neg_mean = sb("neg_mean", [P, 1])
        u_slot = sb("u_slot", [P, TILES])
        comb4 = sb("comb4", [P, TILES, EPG])
        n_last = sb("n_last", [1, 1], I32)
        ps = ctx.enter_context(nc.psum_tensor("ps", [P, 8, 512], F32))

        def stage(name, tensors):
            with ExitStack() as s:
                return {k: s.enter_context(nc.sbuf_tensor(f"{name}_{k}", shape, dt)) for k, (shape, dt) in tensors.items()}

        st_kv = stage("kv", {"mem": ([P, 2, D], F32), "out": ([P, 2, 2, NB], F32)})
        st_mix = []
        for l in range(LAYERS):
            H, V, VB, _ = mixer_shape(l)
            st_mix.append(stage(f"mix{l}", {
                "q": ([P, H, NT], F32), "k": ([P, H, NT], F32), "b": ([P, H, NT], F32),
                "g": ([P, 8, NT], F32), "v": ([P, TILES, D], F32),
                "s": ([P, 8, V], F32), "e": ([P, 2, 4, NT], F32), "t": ([P, 2, NT], F32),
                "dc": ([P, 2, NCH + SAMPLES], F32), "sc": ([P, TILES, P], F32),
                "kn_hi": ([P, TILES, P], F32R), "kn_lo": ([P, TILES, P], F32R), "s0": ([P, SAMPLES, V], F32),
                "sq": ([P, VB, NT], F32), "rn": ([P, NT], F32)}))
        st_att = stage("att", {
            "q": ([P, 8, PROMPT], F32), "qs_hi": ([P, 8, 2, 4, 32], F32R), "qs_lo": ([P, 8, 2, 4, 32], F32R),
            "kt_hi": ([P, 2, 8, MEM], F32R), "kt_lo": ([P, 2, 8, MEM], F32R), "p": ([P, 4, XH, MEM], F32),
            "mx": ([P, 4, XH], F32), "sum": ([P, 4, XH], F32), "rs": ([P, 4, XH], F32)})
        st_in_keys = stage("in_keys", {
            "queries": ([P, 3, 8, PROMPT], F32), "kt": ([P, 8, MEM], F32), "pt": ([P, 2, XH, PROMPT], F32),
            "lo": ([P, 8, MEM], F32), "rows": ([P, 2, D], F32)})
        kt0, pt, o_rows = st_in_keys["kt"], st_in_keys["pt"], st_in_keys["rows"]
        pts_hi, pts_lo = (st_att[k][:, 0].rearrange("p b m -> p (b m)").rearrange("p (r m h s) -> p r m h s", r=2, m=2, h=XH)
                          for k in ("kt_hi", "kt_lo"))
        st_moe = stage("moe", {
            "raw3": ([P, 4, NB], F32), "w_hi3": ([P, 4, NB], F32R), "w_lo3": ([P, 4, NB], F32R),
            "xn_hi": ([P, TILES, D], F32R), "xn_lo": ([P, TILES, D], F32R), "xg": ([P, D], F32),
            "rt": ([EXPERTS, TILES * P], F32),
            "y_hi": ([P, D], F32R), "y_lo": ([P, D], F32R),
            "pick": ([P, TILES, P], F32R), "pick_t": ([P, TILES * P], F32R), "cw": ([P, EPG], F32),
            "sil": ([P, F], F32), "h": ([P, 2, F], F32),
            "ht_hi": ([P, 2, 4, P], F32R), "ht_lo": ([P, 2, 4, P], F32R),
            "sc": ([P, TILES, EXPERTS], F32), "sel": ([P, TILES, EXPERTS], F32),
            "pair": ([P, TILES, GROUPS, 6], F32), "gs": ([P, TILES, GROUPS], F32),
            "gm": ([P, TILES], F32), "g": ([P, TILES, GROUPS], F32),
            "r1": ([P, TILES, EXPERTS], F32), "r2": ([P, TILES, EXPERTS], F32), "r3": ([P, TILES, EXPERTS], F32),
            "m1": ([P, TILES], F32), "pos": ([P, TILES, GROUPS], F32), "p2": ([P, TILES, GROUPS], F32),
            "mc": ([P, 1], F32), "mc2": ([P, 1], F32)})

        loaded = [sem(f"w_loaded{i}") for i in range(MRING)]
        w_high = sem("w_high")
        w_low = sem("w_low")
        w_used = sem("w_used")
        evac = [sem("evac0"), sem("evac1")]
        xt_ps, xt_h, xt_l = sem("xt_ps"), sem("xt_h"), sem("xt_l")
        consts_in, consts = sem("consts_in"), sem("consts")
        ident_made = sem("ident_made")
        mem_in, x_in, x_pad = sem("mem_in"), sem("x_in"), sem("x_pad")
        kv_out = [sem("kv_out0"), sem("kv_out1")]
        ln_pool = sem("ln_pool")
        ln_nm, ln_z = sem("ln_nm"), sem("ln_z")
        ln_in, ln_var, ln_rstd, ln_done = sem("ln_in"), sem("ln_var"), sem("ln_rstd"), sem("ln_done")
        dve_step, act_step, pool_step = sem("dve_step"), sem("act_step"), sem("pool_step")
        y_out = sem("y_out")
        mx_exp, mx_inv, mx_ln, mx_scan = sem("mx_exp"), sem("mx_inv"), sem("mx_ln"), sem("mx_scan")
        mx_lr, mx_lrc, mx_z = sem("mx_lr"), sem("mx_lrc"), sem("mx_z")
        hd_t, hd_e, hd_m = sem("hd_t"), sem("hd_e"), sem("hd_m")
        hd_sc, hd_tr = sem("hd_sc"), sem("hd_tr")
        hd_msk, hd_kn = sem("hd_msk"), sem("hd_kn")
        hd_u, hd_s = sem("hd_u"), sem("hd_s")
        hd_i = sem("hd_i")
        hd_su, hd_ss = sem("hd_su"), sem("hd_ss")
        hd_dec = sem("hd_dec")
        hd_vh, hd_vl, hd_kl = sem("hd_vh"), sem("hd_vl"), sem("hd_kl")
        hd_sq, hd_ms, hd_ln, hd_r = sem("hd_sq"), sem("hd_ms"), sem("hd_ln"), sem("hd_r")
        hd_y, hd_hi, hd_fin = sem("hd_y"), sem("hd_hi"), sem("hd_fin")
        s0_in, s0_out, s_out = sem("s0_in"), sem("s0_out"), sem("s_out")
        at_z, at_qs = sem("at_z"), sem("at_qs")
        at_tr, at_ka, at_kv = sem("at_tr"), sem("at_ka"), sem("at_kv")
        at_sc, at_max, at_exp, at_p = sem("at_sc"), sem("at_max"), sem("at_exp"), sem("at_p")
        at_pt, at_pth, at_pte, at_pv = sem("at_pt"), sem("at_pth"), sem("at_pte"), sem("at_pv")
        at_on, at_ot, at_oh, at_ol = sem("at_on"), sem("at_ot"), sem("at_oh"), sem("at_ol")
        rt_w, rt_c, rt_ps, rt_e, rt_g, rt_pos, rt_n = sem("rt_w"), sem("rt_c"), sem("rt_ps"), sem("rt_e"), sem("rt_g"), sem("rt_pos"), sem("rt_n")
        mo = [{k: sem(f"mo{l}_{k}") for k in (
            "xh", "xl", "side", "read", "p", "step", "xgh", "sil", "h", "t", "hth", "htl", "yh", "yl", "scaled")}
            for l in range(LAYERS)]

        block = ctx.enter_context(nc.Block())

        def parts(r):
            if r < RING:
                return raw[:, r], w_hi[:, r], w_lo[:, r]
            return st_moe["raw3"][:], st_moe["w_hi3"][:], st_moe["w_lo3"][:]

        def masked_values(part, l, h, t):
            V = mixer_shape(l)[1]
            off = (h % 2) * SAMPLES * V if l == 0 else 0
            flat = (w_hi if part == "hi" else w_lo)[:, t].rearrange("p k n -> p (k n)")
            return flat[:, off:off + 8 * V]

        def chunk_of(w, col, half):
            return w[half * 512:(half + 1) * 512, col:col + NB].rearrange("(k p) n -> p k n", p=P)

        def block_source(db):
            if db < KV_BLOCKS:
                return a["xattn_w_kv"][db // 4], (db % 4) * NB
            l = 0 if db < BLOCKS0 else 1
            n = db - first_block(l)
            if n < IN_BLOCKS[l]:
                kind, c = block_kind(l, n)
                if l == 0:
                    return a["hgrn_w_in"][0], {"q": 0, "f": 1024, "v": 2048, "gate": 3072}[kind] + c * NB
                return a["gla_w_in"][0], {"q": 0, "k": 512, "v": 1024, "gate": 2048}[kind] + c * NB
            n -= IN_BLOCKS[l]
            w = (a["hgrn_w_out" if l == 0 else "gla_w_out"][0], a["xattn_w_q"][l], a["xattn_w_o"][l])[n // 2]
            return w, (n % 2) * NB

        @block.sync
        def _(sp):
            def load(k, groups, src, dst=None):
                l = 0 if k < CHUNKS0 else 1
                n = k - RING - keys_no(l)
                if k >= CHUNKS0 and k - CHUNKS0 < RING:
                    sp.wait_ge(w_low, at(k - MRING + 1, groups, GCH))
                elif 0 <= n < BATCHES:
                    sp.wait_ge(at_tr, 4 * (BATCHES * l + n + 1))
                elif k >= RING:
                    sp.wait_ge(w_low, at(k - RING + 1, groups, GCH))
                sp.dma_start(raw[:, slot_of(k)] if dst is None else dst, src).then_inc(loaded[slot_of(k)], 16)

            def dense(first, last, groups):
                for k in range(first, last):
                    l = 0 if k < CHUNKS0 else 1
                    n = k - keys_no(l)
                    if 0 <= n < KV_CHUNKS:
                        kind, n = ("k", n) if n < BATCHES else ("v", n - BATCHES)
                        if n == 0:
                            for par in range(2):
                                sp.wait_ge(kv_out[par], 16 * KV_BLOCKS // 2)
                            src = a["mem_k_prompt" if kind == "k" else "mem_v_prompt"][l, 0]
                        else:
                            src = a["cache_mem_" + kind][l, n - 1]
                        src = src.rearrange("(t p) (u h) d -> p t u (h d)", p=P, u=2)
                        sp_dst = raw[:, slot_of(k)].rearrange("p (t u) c -> p t u c", u=2)
                        load(k, groups, src, sp_dst)
                    else:
                        db = (k - l * KV_CHUNKS - (KV_CHUNKS if n >= KV_CHUNKS else 0)) // 2
                        w, col = block_source(db)
                        load(k, groups, chunk_of(w, col, k % 2))

            def group(l, base, groups, g, first):
                for j, (what, e, half) in enumerate(MOE_ORDER):
                    w = a["moe_w_" + what][l]
                    expert = g * EPG + e
                    if isinstance(g, int):
                        w = w[expert]
                    else:
                        w = w[bass.ds(expert, 1)].rearrange("a r c -> (a r) c")
                    src = chunk_of(w, half * NB, 0) if what == "down" else chunk_of(w, 0, half)
                    sp.wait_ge(w_low, at(base if first and j < MRING else base + j - MRING + 1, groups, GCH))
                    sp.dma_start(parts(j % MRING)[0], src).then_inc(loaded[j % MRING], 16)

            sp.dma_start(st_kv["mem"][:, :, :], a["mem_prompt"][0].rearrange("(t p) c -> p t c", p=P)).then_inc(mem_in, 16)
            for k in range(3):
                w, col = block_source(k // 2)
                load(k, None, chunk_of(w, col, k % 2))
            sp.dma_start(x[:, 0:2, :], a["x_prompt"][0].rearrange("(t p) c -> p t c", p=P)).then_inc(x_in, 16)
            sp.dma_start(x[0:64, 2, :], a["x_sample"].rearrange("b t c -> (b t) c")).then_inc(x_in, 16)
            groups = None
            done = 3
            for l in range(LAYERS):
                H, V, VB, _ = mixer_shape(l)
                m = st_mix[l]
                dense(done, in_end(l) + RING, groups)
                done = in_end(l) + RING
                s_in = a["state_hgrn" if l == 0 else "state_gla"][0]
                s_new = a["state_hgrn_sample" if l == 0 else "state_gla_sample"][0]
                s_fin = a["state_hgrn_prompt" if l == 0 else "state_gla_prompt"][0, 0]
                h0 = l * 8
                for h in range(H):
                    if h == 0:
                        sp.wait_ge(mx_scan, l * 8 + 1)
                    else:
                        sp.wait_ge(s0_out, 16 * (h0 + h))
                    sp.dma_start(m["s0"][:, :, :], s_in[:, h].rearrange("b k v -> k b v")).then_inc(s0_in, 16)
                    sp.wait_ge(hd_s, NCH * (h0 + h + 1))
                    sp.dma_start(s_fin[h], m["s"][:, (NCH - 1) % 8, :]).then_inc(s_out, 16)
                    sp.wait_ge(hd_ss, SAMPLES * (h0 + h + 1))
                    sp.dma_start(s_new[:, h].rearrange("b k v -> k b v"), m["s0"][:, :, :]).then_inc(s0_out, 16)
                last = CHUNKS0 if l == 0 else CHUNKS1
                dense(done, last, groups)
                done = last
                group(l, last, 0 if groups is None else groups, 0, True)
                sp.wait_ge(rt_n, l + 1)
                nl = sp.value_load(n_last[0:1, 0:1], min_val=3, max_val=11)
                with sp.Fori(1, nl) as i:
                    group(l, last, i if groups is None else groups + i, i % GROUPS, False)
                group(l, last, nl if groups is None else groups + nl, GROUPS - 1, False)
                groups = nl + 1 if groups is None else groups + nl + 1
            sp.wait_ge(s_out, 16 * 12)
            sp.wait_ge(s0_out, 16 * 12)

        @block.gpsimd
        def _(pool):
            steps = [0]

            def link(ins):
                steps[0] += 1
                ins.then_inc(pool_step, 1)
                pool.wait_ge(pool_step, steps[0])

            small = [(gain_a[:, :], a["hgrn_norm_g"].rearrange("o p -> p o")),
                     (gain_b[:, :], a["gla_norm_g"].rearrange("o (c p) -> p (o c)", p=P)),
                     (b_gk[:, :], a["gla_b_gk2"].rearrange("o (c p) -> p (o c)", p=P)),
                     (w_gk[:, :], a["gla_w_gk2"][0]),
                     (w_lr[:, :, :], a["gla_w_in"][0][:, 3072:3088].rearrange("(k p) n -> p k n", p=P)),
                     (router[:, :, :], a["router_w"].rearrange("(k p) n -> p k n", p=P)),
                     (r_bias[:, :], a["router_bias"].partition_broadcast(P))]
            small += [(lb_rows[:, r, :], a["hgrn_lb_logits"][r].rearrange("(h p) -> p h", p=P)) for r in range(3)]
            with nc.allow_non_contiguous_dma(reason="a few hundred words, once"):
                for dst, src in small:
                    pool.dma_start(dst, src).then_inc(consts_in, 16)

            def select(t, fill, base, pattern, mult, op=ALU.is_ge):
                link(nc.gpsimd.affine_select(out=t, in_=t, compare_op=op, fill=fill, base=base,
                                             pattern=pattern, channel_multiplier=mult))
            link(nc.gpsimd.memset(ident[:], 0.0))
            select(ident[:], 1.0, 0, [[-1, P]], 1, ALU.not_equal)
            nc.gpsimd.sem_inc(ident_made, 1)
            nc.gpsimd.memset(ones[:], 1.0)
            nc.gpsimd.memset(eps[:], RMS_EPS)
            link(nc.gpsimd.memset(before[:], 1.0))
            select(before[:], 0.0, -1, [[1, P]], -1)
            link(nc.gpsimd.iota(slot_no[:], [[1, P]], base=0, channel_multiplier=0, allow_small_or_imprecise_dtypes=True))
            link(nc.gpsimd.iota(g_base[:], [[P, GROUPS]], base=1, channel_multiplier=0, allow_small_or_imprecise_dtypes=True))
            link(nc.gpsimd.iota(e_rank[:], [[-1, EXPERTS]], base=EXPERTS, channel_multiplier=0, allow_small_or_imprecise_dtypes=True))
            link(nc.gpsimd.memset(mask_f[:], 1.0))
            view = mask_f[:].rearrange("p (c i) -> p c i", i=CH)
            select(view, 0.0, 0, [[CH, P // CH], [1, CH]], -1)
            select(view, 0.0, 0, [[-CH, P // CH], [0, CH]], 1)
            link(nc.gpsimd.tensor_copy(mask16[:], mask_f[:]))
            link(nc.gpsimd.memset(mask_f[:], 1.0))
            view = mask_f[:, 0:64].rearrange("p (c i) -> p c i", i=8)
            select(view, 0.0, 0, [[8, 8], [1, 8]], -1)
            select(view, 0.0, 0, [[-8, 8], [0, 8]], 1)
            link(nc.gpsimd.tensor_copy(mask8[:], mask_f[:, 0:64]))
            link(nc.gpsimd.memset(carry[:], 1.0))
            link(nc.gpsimd.memset(carry[:, 0:PROMPT].rearrange("p (c i) -> p c i", i=CH)[:, :, 0:1], 0.0))
            link(nc.gpsimd.memset(carry[:, PROMPT:NT].rearrange("p (c i) -> p c i", i=8)[:, :, 0:1], 0.0))
            link(nc.gpsimd.memset(batch_of[:], 0.0))
            view = batch_of[:].rearrange("p (b i) -> p b i", i=32)
            select(view, 1.0, 0, [[0, 4], [-1, 32]], 1, ALU.not_equal)
            select(view, 0.0, 0, [[-8, 4], [0, 32]], 1)
            select(view, 0.0, 7, [[8, 4], [0, 32]], -1)
            link(nc.gpsimd.memset(mask_f[:], 1.0))
            select(mask_f[:, 0:8], 0.0, 0, [[-16, 8]], 1)
            select(mask_f[:, 0:8], 0.0, 15, [[16, 8]], -1)
            select(mask_f[:, 16:32], 0.0, 0, [[-8, 16]], 1)
            select(mask_f[:, 16:32], 0.0, 7, [[8, 16]], -1)
            nc.gpsimd.sem_inc(consts, 1)

            for db in range(KV_BLOCKS):
                par, l, c = db % 2, db // 4, db % 4
                pool.wait_ge(evac[par], db // 2 + 1)
                dst = a["mem_k_prompt" if c < 2 else "mem_v_prompt"][l, 0].rearrange("(t p) h d -> p t (h d)", p=P)
                pool.dma_start(dst[:, :, (c % 2) * NB:(c % 2 + 1) * NB], st_kv["out"][:, par]).then_inc(kv_out[par], 16)

            def load_ln(q):
                if q:
                    pool.wait_ge(ln_done, TILES * q)
                pool.dma_start(ln_gb[:, 0, :], a["ln_g"][q // 3, q % 3].partition_broadcast(P)).then_inc(ln_in, 16)
                pool.dma_start(ln_gb[:, 1, :], a["ln_b"][q // 3, q % 3].partition_broadcast(P)).then_inc(ln_in, 16)

            def head_gates(l, h):
                H, V, VB, _ = mixer_shape(l)
                m, n = st_mix[l], l * 8 + h
                b = m["b"][:, h, :]
                bp, bs = b[:, 0:PROMPT].rearrange("p (c i) -> p c i", i=CH), b[:, PROMPT:NT].rearrange("p (c i) -> p c i", i=8)
                pool.wait_ge(mx_scan, n + 1)
                if h:
                    pool.wait_ge(hd_e, n)
                for r, (lo, hi) in enumerate(((CH // 2, 4), (CH - 1, 7))):
                    tp = m["t"][:, r, 0:PROMPT].rearrange("p (c i) -> p c i", i=CH)
                    ts = m["t"][:, r, PROMPT:NT].rearrange("p (c i) -> p c i", i=8)
                    rp, rs = bp[:, :, lo:lo + 1].to_broadcast([P, NCH, CH]), bs[:, :, hi:hi + 1].to_broadcast([P, 8, 8])
                    if r == 0:
                        nc.gpsimd.tensor_tensor(tp, bp, rp, ALU.subtract)
                        nc.gpsimd.tensor_tensor(ts, bs, rs, ALU.subtract)
                    else:
                        nc.gpsimd.tensor_tensor(tp, rp, bp, ALU.subtract)
                        nc.gpsimd.tensor_tensor(ts, rs, bs, ALU.subtract).then_inc(hd_t, 1)

            def head_products(l, h):
                m, n = st_mix[l], l * 8 + h
                pool.wait_ge(hd_e, n + 1)
                e = m["e"][:, h % 2]
                for r, src in enumerate(("q", "k", "q", "k")):
                    ins = nc.gpsimd.tensor_tensor(e[:, r, :], e[:, r, :], m[src][:, h, :], ALU.mult)
                ins.then_inc(hd_m, 1)

            def head_values(l, h, tiles):
                H, V, VB, _ = mixer_shape(l)
                m, n = st_mix[l], l * 8 + h
                for t in tiles:
                    rows = P if t < 2 else 64
                    if l == 1 and h:
                        pool.wait_ge(hd_su if t == 2 else hd_u, fills(l, h, True) if t == 2 else fills(l, h - 1, False) + 4 * (t + 1))
                    elif h >= 2 and t == 0:
                        pool.wait_ge(hd_su, fills(l, h - 1, True))
                    mask = mask_f[0:rows, 0:8] if t < 2 else mask_f[0:rows, 16:24]
                    nc.gpsimd.tensor_tensor(masked_values("hi", l, h, t)[0:rows].rearrange("p (c v) -> p c v", c=8),
                                            m["v"][0:rows, t, h * V:(h + 1) * V].unsqueeze(1).to_broadcast([rows, 8, V]),
                                            mask.unsqueeze(2).to_broadcast([rows, 8, V]), ALU.mult).then_inc(hd_vh, 1)

            def head_decay(l, h):
                H, V, VB, _ = mixer_shape(l)
                m, n = st_mix[l], l * 8 + h
                pool.wait_ge(hd_i, 15 * n + 1)
                nc.gpsimd.tensor_tensor(m["s0"][:], m["s0"][:], m["dc"][:, h % 2, NCH:NCH + 8].unsqueeze(2).to_broadcast([P, SAMPLES, V]),
                                        ALU.mult).then_inc(hd_dec, 1)

            def head_low(l, h):
                H, V, VB, _ = mixer_shape(l)
                m, n = st_mix[l], l * 8 + h
                pool.wait_ge(hd_hi, n + 1)
                nc.gpsimd.tensor_tensor(xt_lo[:, h * VB:(h + 1) * VB, 0:NT], m["sq"][:],
                                        xt_hi[:, h * VB:(h + 1) * VB, 0:NT].bitcast(F32), ALU.subtract).then_inc(hd_fin, 1)

            def layer_norm(q):
                t = TILES - 1
                pool.wait_ge(ln_in, 32 * (q + 1))
                pool.wait_ge(ln_z, q + 1)
                nc.gpsimd.tensor_tensor(x[:, t, :], x[:, t, :], ln_gb[:, 0, :], ALU.mult).then_inc(ln_pool, 1)
                pool.wait_ge(ln_pool, q + 1)
                nc.gpsimd.tensor_tensor(x[:, t, :], x[:, t, :], ln_gb[:, 1, :], ALU.add).then_inc(ln_done, 1)

            groups = None
            for l in range(LAYERS):
                H, V, VB, _ = mixer_shape(l)
                load_ln(3 * l)
                head_gates(l, 0)
                head_products(l, 0)
                head_gates(l, 1)
                for d in (1, 2):
                    db = first_block(l) + IN_BLOCKS[l] - d
                    pool.wait_ge(evac[db % 2], db // 2 + 1)
                pool.wait_ge(w_used, at(in_end(l), groups, GCH))
                head_values(l, 0, (0, 1, 2))
                for h in range(H):
                    if h + 1 < H:
                        head_values(l, h + 1, (0, 1))
                        head_products(l, h + 1)
                    if h + 2 < H:
                        head_gates(l, h + 2)
                    head_decay(l, h)
                    if h + 1 < H:
                        head_values(l, h + 1, (2,))
                    head_low(l, h)
                pool.wait_ge(hd_fin, l * 8 + H)
                pool.wait_ge(s0_out, 16 * (l * 8 + H))
                pool.wait_ge(s_out, 16 * (l * 8 + H))
                for part in ("qs_hi", "qs_lo"):
                    ins = nc.gpsimd.tensor_scalar(st_att[part][:].rearrange("p c r b i -> p (c r b i)").rearrange("p (n s) -> p n s", s=P),
                                                  ones[:].unsqueeze(1).to_broadcast([P, 16, P]), 0.0, None, ALU.mult)
                ins.then_inc(at_z, 1)
                layer_norm(3 * l)
                load_ln(3 * l + 1)
                layer_norm(3 * l + 1)
                load_ln(3 * l + 2)
                pool.wait_ge(mo[l]["xh"], 1)
                nc.gpsimd.tensor_tensor(st_moe["xn_lo"][:], x[:], st_moe["xn_hi"][:].bitcast(F32), ALU.subtract).then_inc(mo[l]["xl"], 1)
                pool.wait_ge(mo[l]["xl"], 1)
                nc.gpsimd.tensor_scalar(x[:], x[:], ALPHA, None, ALU.mult).then_inc(mo[l]["scaled"], 1)
                if l == 0:
                    pool.wait_ge(rt_n, 1)
                    groups = pool.value_load(n_last[0:1, 0:1], min_val=3, max_val=11) + 1
                    rw, hi, lo = parts(slot_of(CHUNKS0))
                    pool.wait_ge(w_high, at(CHUNKS0 + 1, groups, GCH))
                    nc.gpsimd.tensor_tensor(lo, rw, hi.bitcast(F32), ALU.subtract).then_inc(w_low, 1)
                layer_norm(3 * l + 2)
                if l == LAYERS - 1:
                    pool.wait_ge(ln_done, TILES * 6)
                    pool.dma_start(a["y_prompt"][0].rearrange("(t p) c -> p t c", p=P), x[:, 0:2, :]).then_inc(y_out, 16)
                    pool.dma_start(a["y_sample"].rearrange("b t c -> (b t) c"), x[0:64, 2, :]).then_inc(y_out, 16)
                    pool.wait_ge(y_out, 32)

        @block.scalar
        def _(act):
            splits = [0]

            def split(k, groups):
                r = slot_of(k)
                act.wait_ge(loaded[r], at(16 * loads_of(k), groups, 16 * GCH // MRING))
                if k >= CHUNKS0 and k - CHUNKS0 < RING:
                    act.wait_ge(w_used, at(CHUNKS0, groups, GCH))
                elif k >= RING:
                    act.wait_ge(w_used, at(k - RING + 1, groups, GCH))
                nc.scalar.activation(w_hi[:, r], raw[:, r], ACT.Copy).then_inc(w_high, 1)

            def split_expert(l, j, g, first):
                base, (rw, hi, _) = (CHUNKS0 if l == 0 else CHUNKS1), parts(j % MRING)
                act.wait_ge(loaded[j % MRING], at(16 * moe_loads_of(l, j), g, 16 * GCH // MRING))
                act.wait_ge(w_used, at(base if first and j < MRING else base + j - MRING + 1, g, GCH))
                nc.scalar.activation(hi, rw, ACT.Copy).then_inc(w_high, 1)

            def split_ahead(db, groups):
                while splits[0] < min((chunk_no(db) if db >= 0 else -2) + 5, split_limit(db)):
                    split(splits[0], groups)
                    splits[0] += 1

            def block_out(db, groups, out, ins, func, **kw):
                split_ahead(db, groups)
                act.wait_ge(w_used, at(chunk_no(db) + 2, groups, GCH))
                return nc.scalar.activation(out, ins, func, **kw)

            def transposed(u, tiles):
                for kt in range(KT):
                    act.wait_ge(xt_ps, 8 * u + kt + 1)
                    nc.scalar.activation(xt_hi[:, kt, 0:tiles * P], ps[:, kt % 4, 0:tiles * P], ACT.Copy).then_inc(xt_h, 1)

            def layer_norm(q):
                act.wait_ge(ln_var, q + 1)
                nc.scalar.activation(rstd[:], rstd[:], ACT.Ln).then_inc(act_step, 1)
                act.wait_ge(act_step, q + 1)
                nc.scalar.activation(rstd[:], rstd[:], ACT.Exp, scale=-0.5).then_inc(ln_rstd, 1)
                t = TILES - 1
                act.wait_ge(ln_nm, q + 1)
                act.wait_ge(ln_rstd, q + 1)
                nc.scalar.activation(x[:, t, :], x[:, t, :], ACT.Identity, bias=neg_mean[:, 0:1], scale=rstd[:, t:t + 1]).then_inc(ln_z, 1)

            def sigmoid(db, groups, dst):
                block_out(db, groups, dst, ps[:, 4 * (db % 2):4 * (db % 2) + 4, 0:NT], ACT.Sigmoid).then_inc(mx_exp, 1)

            def head(l, h):
                H, V, VB, gs = mixer_shape(l)
                m, n = st_mix[l], l * 8 + h
                if h >= 2:
                    act.wait_ge(hd_i, 15 * (n - 1))
                act.wait_ge(hd_t, n + 1)
                e, t, b = m["e"][:, h % 2], m["t"], m["b"][:, h, :]
                nc.scalar.activation(e[:, 0, :], t[:, 0, :], ACT.Exp, scale=gs)
                nc.scalar.activation(e[:, 1, :], t[:, 0, :], ACT.Exp, scale=-gs)
                nc.scalar.activation(e[:, 2, :], b, ACT.Exp, scale=gs)
                nc.scalar.activation(e[:, 3, :], t[:, 1, :], ACT.Exp, scale=gs)
                nc.scalar.activation(m["dc"][:, h % 2, 0:NCH], b[:, CH - 1:PROMPT:CH], ACT.Exp, scale=gs)
                nc.scalar.activation(m["dc"][:, h % 2, NCH:NCH + 8], b[:, PROMPT + 7:NT:8], ACT.Exp, scale=gs).then_inc(hd_e, 1)

            def head_keys(l, h):
                m, n = st_mix[l], l * 8 + h
                act.wait_ge(hd_tr, n + 1)
                nc.scalar.activation(m["kn_hi"][:, 0:2, :], ps[:, 1, 0:PROMPT].rearrange("p (t k) -> p t k", t=2), ACT.Copy)
                nc.scalar.activation(m["kn_hi"][0:64, 2, :], ps[0:64, 1, PROMPT:PROMPT + P], ACT.Copy).then_inc(hd_kn, 1)

            def head_norm(l, h):
                H, V, VB, gs = mixer_shape(l)
                m, n = st_mix[l], l * 8 + h
                act.wait_ge(hd_i, 15 * (n + 1))
                if h:
                    act.wait_ge(hd_fin, n)
                nc.scalar.activation(m["sq"][:], ps[:, 6:6 + VB, 0:NT], ACT.Square).then_inc(hd_sq, 1)
                if h + 1 < H:
                    head_keys(l, h + 1)
                else:
                    act.wait_ge(hd_su, fills(l, H, True))
                    split(splits[0], groups)
                    splits[0] += 1
                act.wait_ge(hd_ms, n + 1)
                nc.scalar.activation(m["rn"][:], ps[:, 5, 0:NT], ACT.Ln, bias=eps[:, 0:1], scale=1.0 / V).then_inc(hd_ln, 1)
                act.wait_ge(hd_ln, n + 1)
                nc.scalar.activation(m["rn"][:], m["rn"][:], ACT.Exp, scale=-0.5).then_inc(hd_r, 1)
                if h + 2 < H:
                    head(l, h + 2)
                act.wait_ge(hd_y, n + 1)
                nc.scalar.activation(xt_hi[:, h * VB:(h + 1) * VB, 0:NT], m["sq"][:], ACT.Copy).then_inc(hd_hi, 1)

            nc.scalar.preload_act_table_set("natural_log_exp_and_others")
            split_ahead(-1, None)
            transposed(0, 2)
            for db in range(KV_BLOCKS):
                par = db % 2
                if db >= 2:
                    act.wait_ge(kv_out[par], 16 * (db // 2))
                block_out(db, None, st_kv["out"][:, par], ps[:, 4 * par:4 * par + 2, :], ACT.Copy).then_inc(evac[par], 1)
            transposed(1, TILES)
            act.wait_ge(consts_in, 160)
            nc.scalar.activation(r_hi[:], router[:], ACT.Copy).then_inc(rt_w, 1)
            act.wait_ge(consts, 4)
            nc.scalar.activation(lb_rows[:], lb_rows[:], ACT.Exp).then_inc(consts, 1)
            groups = None
            for l in range(LAYERS):
                H, V, VB, gs = mixer_shape(l)
                m = st_mix[l]
                if l == 0:
                    for par in range(2):
                        act.wait_ge(kv_out[par], 16 * KV_BLOCKS // 2)
                for nb in range(IN_BLOCKS[l]):
                    db = first_block(l) + nb
                    par = db % 2
                    kind, c = block_kind(l, nb)
                    four = ps[:, 4 * par:4 * par + 4, 0:NT]
                    e_dst = m["e"][:, c % 2]
                    if kind == "f":
                        sigmoid(db, groups, m["b"][:, 4 * c:4 * c + 4, :])
                    elif kind == "q" and l == 0:
                        sigmoid(db, groups, e_dst)
                    elif kind == "gate":
                        if l == 0:
                            act.wait_ge(mx_inv, 3 + c)
                        elif c == 1:
                            act.wait_ge(mx_inv, 9)
                        sigmoid(db, groups, e_dst)
                    elif kind in ("q", "k"):
                        block_out(db, groups, m[kind][:], four, ACT.Copy,
                                  scale=float(P) ** -0.5 if kind == "q" else 1.0).then_inc(evac[par], 1)
                    else:
                        block_out(db, groups, m["v"][:, :, c * NB:(c + 1) * NB], ps[:, 4 * par:4 * par + 3, :], ACT.Copy)\
                            .then_inc(evac[par], 1)
                    if kind == "gate" and c == 1:
                        nc.scalar.preload_act_table_set("natural_log_exp_and_others")
                    if l == 0 and kind == "gate" and c == 1:
                        for f in range(2):
                            act.wait_ge(mx_inv, f + 1)
                            nc.scalar.activation(m["b"][:, 4 * f:4 * f + 4, :], m["b"][:, 4 * f:4 * f + 4, :], ACT.Ln).then_inc(mx_ln, 1)
                    if l == 1 and kind == "k":
                        act.wait_ge(mx_lr, 1)
                        nc.scalar.activation(lr_t[:], ps[0:16, 3, 0:NT], ACT.Copy).then_inc(mx_lrc, 1)
                        for hh in range(4):
                            act.wait_ge(mx_z, hh + 1)
                            nc.scalar.activation(m["b"][:, hh, :], ps[:, hh % 2, 0:NT], ACT.Abs, bias=b_gk[:, hh:hh + 1]).then_inc(mx_lrc, 1)
                        act.wait_ge(mx_lrc, 5)
                        nc.scalar.activation(m["b"][:], m["b"][:], ACT.Exp, scale=-1.0).then_inc(mx_lrc, 1)
                        act.wait_ge(mx_lrc, 6)
                        nc.scalar.activation(m["b"][:], m["b"][:], ACT.Ln, bias=1.0).then_inc(mx_ln, 1)
                head(l, 0)
                head_keys(l, 0)
                head(l, 1)
                for h in range(H):
                    head_norm(l, h)
                db = first_block(l) + IN_BLOCKS[l]
                split_ahead(db, groups)
                split_ahead(db + 1, groups)
                layer_norm(3 * l)
                transposed(2 + 3 * l, TILES)
                act.wait_ge(at_z, l + 1)
                t_ = st_att
                for c in range(2):
                    d2 = db + 2 + c
                    b4 = 4 * (d2 % 2)
                    block_out(d2, groups, t_["q"][:, 4 * c:4 * c + 4, :], ps[:, b4:b4 + 4, 0:PROMPT], ACT.Copy)
                    for b in range(4):
                        ins = nc.scalar.activation(t_["qs_hi"][:, 4 * c:4 * c + 4, :, b, 8 * b:8 * b + 8],
                                                   ps[:, b4:b4 + 4, PROMPT:NT].rearrange("p c (r b i) -> p c r b i", r=2, b=4)[:, :, :, b, :], ACT.Copy)
                    ins.then_inc(at_qs, 1)

                def keys_out(n):
                    for s in ((0, 2) if n == 0 else range(4)):
                        act.wait_ge(at_tr, 4 * (BATCHES * l + n) + s + 1)
                        if n >= 2:
                            act.wait_ge(at_sc, BATCHES * l + n - 1)
                        out = kt0[:, 2 * s:2 * s + 2, :] if n == 0 else t_["kt_hi"][:, n % 2, 2 * s:2 * s + 2, :]
                        nc.scalar.activation(out, ps[:, s % 2, :].rearrange("p (b m) -> p b m", b=2),
                                             ACT.Copy).then_inc(at_ka, 1)

                def exps(t, banks):
                    rows = P if t < 2 else 32
                    act.wait_ge(at_max, 4 * l + t + 1)
                    s = ps[0:rows, banks:banks + 2, :].rearrange("p a (b m) -> p (a b) m", b=2)
                    for hh in range(XH):
                        ins = nc.scalar.activation(t_["p"][0:rows, t, hh, :], s[:, hh, :], ACT.Exp,
                                                   bias=t_["mx"][0:rows, t, hh:hh + 1], scale=float(D // XH) ** -0.5,
                                                   accum_out=t_["sum"][0:rows, t, hh:hh + 1])
                    ins.then_inc(at_exp, 1)

                def split_values(n):
                    k = keys_no(l) + BATCHES + n
                    act.wait_ge(loaded[slot_of(k)], at(16 * loads_of(k), groups, 16 * GCH // MRING))
                    act.wait_ge(w_used, at(keys_no(l) if n <= RING else k - RING + 1, groups, GCH))
                    nc.scalar.activation(w_hi[:, slot_of(k)], raw[:, slot_of(k)], ACT.Copy).then_inc(w_high, 1)

                keys_out(0)
                keys_out(1)
                exps(0, 4)
                keys_out(2)
                exps(1, 6)
                for n in range(3, 7):
                    keys_out(n)
                exps(2, 2)
                keys_out(7)
                keys_out(8)
                act.wait_ge(at_sc, BATCHES * (l + 1))
                for r in range(4):
                    act.wait_ge(at_pt, 8 * l + r + 1)
                    nc.scalar.activation(pt[:, r % 2, :, (r // 2) * P:(r // 2 + 1) * P],
                                         ps[:, (0, 1, 6, 7)[r], :].rearrange("p (h q) -> p h q", h=XH), ACT.Copy).then_inc(at_pte, 1)
                exps(3, 4)
                split_values(1)
                for r in range(2):
                    for mh in range(2):
                        act.wait_ge(at_pt, 8 * l + 4 + 2 * r + mh + 1)
                        nc.scalar.activation(pts_hi[:, r, mh], ps[:, 6 - 2 * r + mh, :].rearrange("p (h s) -> p h s", h=XH), ACT.Copy).then_inc(at_pth, 1)
                    if r == 0:
                        for c in range(2):
                            act.wait_ge(at_pv, 2 * l + c + 1)
                            nc.scalar.activation(xt_hi[:, 4 * c:4 * c + 4, 0:PROMPT], ps[:, 2 - 2 * c:4 - 2 * c, :].rearrange("p a (b q) -> p (a b) q", b=2),
                                                 ACT.Copy).then_inc(at_oh, 1)
                        split_values(2)
                split_values(3)

                def rows_out(r):
                    act.wait_ge(w_used, at(keys_no(l) + BATCHES + 4 * (r + 1) + 1, groups, GCH))
                    nc.scalar.activation(o_rows[0:32, r, :].rearrange("p (a c) -> p a c", a=2), ps[0:32, 6 - 2 * r:8 - 2 * r, :], ACT.Copy).then_inc(at_on, 1)

                def rows_back(r):
                    act.wait_ge(at_ot, 2 * l + r + 1)
                    nc.scalar.activation(xt_hi[:, :, PROMPT + 32 * r:PROMPT + 32 * r + 32], ps[:, 2 - 2 * r, 0:256].rearrange("p (k s) -> p k s", k=8),
                                         ACT.Copy).then_inc(at_oh, 1)

                for n in range(4, 8):
                    split_values(n)
                rows_out(0)
                split_values(8)
                rows_back(0)
                splits[0] = chunk_no(db + 4)
                for _ in range(2):
                    split(splits[0], groups)
                    splits[0] += 1
                rows_out(1)
                rows_back(1)
                split_ahead(db + 4, groups)
                split_ahead(db + 5, groups)
                layer_norm(3 * l + 1)
                transposed(3 + 3 * l, TILES)
                m, s = st_moe, mo[l]
                nc.scalar.activation(m["xn_hi"][:], x[:], ACT.Copy).then_inc(s["xh"], 1)
                g0 = 0 if groups is None else groups
                act.wait_ge(rt_ps, 2 * l + 1)
                nc.scalar.activation(m["rt"][:], ps[0:EXPERTS, 4, 0:TILES * P], ACT.Copy).then_inc(rt_c, 1)
                act.wait_ge(rt_ps, 2 * l + 2)
                nc.scalar.activation(m["sc"][:].rearrange("p t e -> p (t e)"), ps[:, 5, 0:TILES * EXPERTS], ACT.Exp, scale=-1.0).then_inc(rt_e, 1)
                for j in range(MRING):
                    split_expert(l, j, g0, True)

                def side(i, what, n, k):
                    if what == "s":
                        return
                    act.wait_ge(s["side"], k)
                    bank = ps[:, 7, :]
                    if what == "cw":
                        nc.scalar.activation(m["cw"][:], bank[:, 0:EPG], ACT.Copy).then_inc(s["read"], 1)
                    elif what == "pt":
                        nc.scalar.activation(m["pick_t"][:], bank[:, 0:TILES * P], ACT.Copy).then_inc(s["read"], 1)
                    elif what == "g":
                        nc.scalar.activation(m["xg"][:, n * NB:(n + 1) * NB], bank, ACT.Copy).then_inc(s["read"], 1)
                    else:
                        nc.scalar.activation(xt_hi[:, 4 * n:4 * n + 4, 0:P], bank.rearrange("p (k s) -> p k s", k=4), ACT.Copy).then_inc(s["xgh"], 1)

                def sums_out(g):
                    act.wait_ge(w_used, at(base, g, GCH))
                    nc.scalar.activation(m["y_hi"][:].rearrange("p (a c) -> p a c", a=2), ps[:, 4:6, :], ACT.Copy).then_inc(s["yh"], 1)

                def visit(i, first, last_one):
                    g = i if groups is None else groups + i
                    if not first:
                        sums_out(g)
                    uses = side_order(first, last_one)
                    for j in range(GCH):
                        for e in range(EPG):
                            if j == GU_LAST[e]:
                                act.wait_ge(w_used, at(base + j + 1, g, GCH))
                                act.wait_ge(s["h"], i * EPG + e + 1)
                                nc.scalar.activation(m["sil"][:], ps[:, 2 * (e % 2), :], ACT.Silu).then_inc(s["sil"], 1)
                        if j in T_AFTER:
                            e = T_AFTER[j]
                            act.wait_ge(s["t"], i * EPG + e + 1)
                            nc.scalar.activation(m["ht_hi"][:, e % 2], ps[:, 6, :].rearrange("p (k s) -> p k s", k=4), ACT.Copy).then_inc(s["hth"], 1)
                        for k, (jj, what, n) in enumerate(uses):
                            if max(jj, 0) == j:
                                side(i, what, n, side_start(i) + k + 1)
                        if j + MRING < GCH or not last_one:
                            split_expert(l, j + MRING, g, False)

                for k, (what, n) in enumerate((("g", 0), ("g", 1), ("t", 0), ("t", 1))):
                    side(0, what, n, SKIPPED + k + 1)
                base = CHUNKS0 if l == 0 else CHUNKS1
                visit(0, True, False)
                act.wait_ge(rt_n, l + 1)
                nl = act.value_load(n_last[0:1, 0:1], min_val=3, max_val=11)
                with act.Fori(1, nl) as i:
                    visit(i, False, False)
                visit(nl, False, True)
                groups = nl + 1 if groups is None else groups + nl + 1
                sums_out(groups)
                if l == 0:
                    for k in range(RING):
                        split(CHUNKS0 + k, groups)
                    splits[0] += RING
                nc.scalar.preload_act_table_set("natural_log_exp_and_others")
                layer_norm(3 * l + 2)
                if l == 0:
                    transposed(4, TILES)

        @block.vector
        def _(dve):
            splits, steps = [0], [0]

            def link(ins):
                steps[0] += 1
                ins.then_inc(dve_step, 1)
                dve.wait_ge(dve_step, steps[0])

            def split(k, groups, r=None):
                rw, hi, lo = parts(slot_of(k) if r is None else r)
                dve.wait_ge(w_high, at(k + 1, groups, GCH))
                nc.vector.tensor_tensor(lo, rw, hi.bitcast(F32), ALU.subtract).then_inc(w_low, 1)

            def split_ahead(db, groups):
                while splits[0] < min((chunk_no(db) if db >= 0 else -2) + 5, split_limit(db)):
                    split(splits[0], groups)
                    splits[0] += 1

            def block_done(db, groups):
                split_ahead(db, groups)
                dve.wait_ge(w_used, at(chunk_no(db) + 2, groups, GCH))

            def transposed(u, tiles):
                for kt in range(KT):
                    dve.wait_ge(xt_h, 8 * u + kt + 1)
                    nc.vector.tensor_tensor(xt_lo[:, kt, 0:tiles * P], ps[:, kt % 4, 0:tiles * P],
                                            xt_hi[:, kt, 0:tiles * P].bitcast(F32), ALU.subtract).then_inc(xt_l, 1)

            def add_block(db, groups, c):
                if c == 0:
                    split_ahead(db, groups)
                dve.wait_ge(w_used, at(chunk_no(db) + 2, groups, GCH))
                par = db % 2
                for t in range(TILES):
                    cols = x[:, t, c * NB:(c + 1) * NB]
                    ins = nc.vector.scalar_tensor_tensor(out=cols, in0=cols, scalar=ALPHA, in1=ps[:, 4 * par + t, :],
                                                         op0=ALU.mult, op1=ALU.add)
                ins.then_inc(evac[par], 1)
                dve.wait_ge(evac[par], db // 2 + 1)
                half_stats(c)

            def half_stats(c):
                for t in range(TILES):
                    ins = nc.vector.bn_stats(stats[:, t, 6 * c:6 * c + 6], x[:, t, c * NB:(c + 1) * NB])
                link(ins)

            def layer_norm(q):
                for t in range(TILES):
                    ins = nc.vector.bn_aggr(mean_var[:, t, :], stats[:, t, :])
                link(ins)
                nc.vector.tensor_scalar(rstd[:], mean_var[:, :, 1], LN_EPS, None, ALU.add).then_inc(ln_var, 1)
                dve.wait_ge(ln_rstd, q + 1)
                t = TILES - 1
                nc.vector.scalar_tensor_tensor(out=neg_mean[:], in0=mean_var[:, t, 0:1], scalar=-1.0, in1=rstd[:, t:t + 1],
                                               op0=ALU.mult, op1=ALU.mult).then_inc(ln_nm, 1)
                dve.wait_ge(ln_in, 32 * (q + 1))
                for t in range(TILES - 1):
                    ins = nc.vector.scalar_tensor_tensor(out=x[:, t, :], in0=x[:, t, :], scalar=mean_var[:, t, 0:1], in1=ln_gb[:, 0, :],
                                                         op0=ALU.subtract, op1=ALU.mult)
                link(ins)
                for t in range(TILES - 1):
                    nc.vector.scalar_tensor_tensor(out=x[:, t, :], in0=x[:, t, :], scalar=rstd[:, t:t + 1], in1=ln_gb[:, 1, :],
                                                   op0=ALU.mult, op1=ALU.add).then_inc(ln_done, 1)
                dve.wait_ge(ln_done, TILES * (q + 1))

            def inverse(t):
                link(nc.vector.tensor_scalar(t, t, 1.0, None, ALU.add))
                link(nc.vector.reciprocal(t, t))

            nc.vector.memset(x[64:P, 2, :], 0.0).then_inc(x_pad, 1)
            split_ahead(-1, None)
            transposed(0, 2)
            for db in range(KV_BLOCKS):
                split_ahead(db, None)
                if db == 1:
                    dve.wait_ge(consts, 1)
                    dve.wait_ge(consts_in, 160)
                    nc.vector.tensor_tensor(lb_tmp[:], lb_rows[:, 0, :], lb_rows[:, 1, :], ALU.max).then_inc(consts, 1)
                    dve.wait_ge(consts, 2)
                    nc.vector.tensor_tensor(lb_tmp[:], lb_tmp[:], lb_rows[:, 2, :], ALU.max).then_inc(consts, 1)
                    dve.wait_ge(consts, 3)
                    nc.vector.tensor_tensor(lb_rows[:], lb_rows[:], lb_tmp[:].unsqueeze(1).to_broadcast([P, 3, 8]), ALU.subtract).then_inc(consts, 1)
            transposed(1, TILES)
            dve.wait_ge(consts, 5)
            link(nc.vector.tensor_tensor(lb_tmp[:], lb_rows[:, 0, :], lb_rows[:, 1, :], ALU.add))
            link(nc.vector.tensor_tensor(lb_tmp[:], lb_tmp[:], lb_rows[:, 2, :], ALU.add))
            link(nc.vector.reciprocal(lb_tmp[:], lb_tmp[:]))
            link(nc.vector.tensor_tensor(lb[:], lb_rows[:, 0, :], lb_tmp[:], ALU.mult))
            link(nc.vector.tensor_scalar(one_m_lb[:], lb[:], -1.0, 1.0, ALU.mult, ALU.add))
            dve.wait_ge(rt_w, 1)
            nc.vector.tensor_tensor(r_lo[:], router[:], r_hi[:].bitcast(F32), ALU.subtract).then_inc(rt_w, 1)
            groups = None
            for l in range(LAYERS):
                H, V, VB, gs = mixer_shape(l)
                m = st_mix[l]
                exps_seen = 6 * l
                if l == 0:
                    for par in range(2):
                        dve.wait_ge(kv_out[par], 16 * KV_BLOCKS // 2)
                nc.vector.memset(m["sc"][:], 0.0)
                for nb in range(IN_BLOCKS[l]):
                    db = first_block(l) + nb
                    par = db % 2
                    kind, c = block_kind(l, nb)
                    split_ahead(db, groups)
                    four = ps[:, 4 * par:4 * par + 4, 0:NT]
                    if kind == "f":
                        exps_seen += 1
                        dve.wait_ge(mx_exp, exps_seen)
                        b4 = m["b"][:, 4 * c:4 * c + 4, :]
                        nc.vector.engine_nop().then_inc(evac[par], 1)
                        for hh in range(4 * c, 4 * c + 4):
                            ins = nc.vector.tensor_scalar(m["b"][:, hh, :], m["b"][:, hh, :], one_m_lb[:, hh:hh + 1], lb[:, hh:hh + 1], ALU.mult, ALU.add)
                        link(ins)
                        nc.vector.tensor_scalar(m["k"][:, 4 * c:4 * c + 4, :], b4, -1.0, 1.0, ALU.mult, ALU.add).then_inc(mx_inv, 1)
                    elif kind == "q" and l == 0:
                        exps_seen += 1
                        dve.wait_ge(mx_exp, exps_seen)
                        for hh in range(4):
                            ins = nc.vector.scalar_tensor_tensor(out=m["q"][:, 4 * c + hh, :], in0=ps[:, 4 * par + hh, 0:NT], scalar=float(P) ** -0.5,
                                                                 in1=m["e"][:, c % 2, hh, :], op0=ALU.mult, op1=ALU.mult)
                        link(ins)
                        nc.vector.engine_nop().then_inc(evac[par], 1)
                        nc.vector.engine_nop().then_inc(mx_inv, 1)
                    elif kind == "gate":
                        exps_seen += 1
                        dve.wait_ge(mx_exp, exps_seen)
                        for hh in range(4):
                            gain = gain_a[:, 0:1] if l == 0 else gain_b[:, hh % 2:hh % 2 + 1]
                            ins = nc.vector.scalar_tensor_tensor(out=m["g"][:, 4 * c + hh, :], in0=ps[:, 4 * par + hh, 0:NT], scalar=gain,
                                                                 in1=m["e"][:, c % 2, hh, :], op0=ALU.mult, op1=ALU.mult)
                        link(ins)
                        nc.vector.engine_nop().then_inc(evac[par], 1)
                    elif kind == "k" and l == 1:
                        for hh in range(4):
                            dve.wait_ge(mx_lrc, hh + 2)
                            ins = nc.vector.tensor_scalar(m["e"][:, 1, hh, :], ps[:, hh % 2, 0:NT], b_gk[:, hh:hh + 1], 0.0, ALU.add, ALU.min)
                            ins.then_inc(mx_inv, 1)
                        dve.wait_ge(mx_inv, 4 + 4)
                        dve.wait_ge(mx_ln, 3)
                        link(nc.vector.scalar_tensor_tensor(out=m["b"][:], in0=m["b"][:], scalar=-1.0, in1=m["e"][:, 1], op0=ALU.mult, op1=ALU.add))
                        nc.vector.engine_nop().then_inc(mx_inv, 1)
                    if l == 0 and kind == "v" and c == 0:
                        dve.wait_ge(mx_ln, 2)
                    if kind == "v" and c == 0:
                        for hh in range(H):
                            nc.vector.tensor_tensor_scan(m["b"][:, hh, :], carry[:], m["b"][:, hh, :], 0.0, ALU.mult, ALU.add).then_inc(mx_scan, 1)
                CPB = NB // V

                def values_low(h, t, chunks=range(8)):
                    rows = P if t < 2 else 64
                    if 0 in chunks:
                        dve.wait_ge(hd_vh, TILES * (l * 8 + h) + t + 1)
                    for c in chunks:
                        cols = slice(c * V, (c + 1) * V)
                        mask = mask_f[0:rows, (0 if t < 2 else 16) + c:(0 if t < 2 else 16) + c + 1]
                        ins = nc.vector.scalar_tensor_tensor(out=masked_values("lo", l, h, t)[0:rows, cols], in0=m["v"][0:rows, t, h * V:(h + 1) * V],
                                                             scalar=mask, in1=masked_values("hi", l, h, t)[0:rows, cols].bitcast(F32),
                                                             op0=ALU.mult, op1=ALU.subtract)
                    if 7 in chunks:
                        ins.then_inc(hd_vl, 1)

                def scores_keys(h):
                    n = l * 8 + h
                    dve.wait_ge(hd_sc, n + 1)
                    for t in range(2):
                        nc.vector.copy_predicated(m["sc"][:, t, :], mask16[:], ps[:, 0, t * P:(t + 1) * P])
                    nc.vector.copy_predicated(m["sc"][0:64, 2, 0:64], mask8[0:64, :], ps[0:64, 0, PROMPT:PROMPT + 64]).then_inc(hd_msk, 1)
                    dve.wait_ge(hd_kn, n + 1)
                    nc.vector.tensor_tensor(m["kn_lo"][:, 0:2, :], ps[:, 1, 0:PROMPT].rearrange("p (t k) -> p t k", t=2),
                                            m["kn_hi"][:, 0:2, :].bitcast(F32), ALU.subtract)
                    nc.vector.tensor_tensor(m["kn_lo"][0:64, 2, :], ps[0:64, 1, PROMPT:PROMPT + P],
                                            m["kn_hi"][0:64, 2, :].bitcast(F32), ALU.subtract).then_inc(hd_kl, 1)

                values_low(0, 0)
                scores_keys(0)
                values_low(0, 1)
                for h in range(H):
                    n = l * 8 + h
                    dc = m["dc"][:, h % 2]

                    def new_state(c):
                        dve.wait_ge(hd_u, fills(l, h, False) + c // CPB + 1)
                        u = ps[:, 2 + (c // CPB) % 4, (c % CPB) * V:(c % CPB + 1) * V]
                        if c >= 8:
                            dve.wait_ge(hd_i, 15 * n + c - 8 + 1)
                        if c == 7 and h:
                            dve.wait_ge(s_out, 16 * n)
                        if c == 0:
                            nc.vector.tensor_copy(m["s"][:, 0, :], u).then_inc(hd_s, 1)
                        else:
                            dve.wait_ge(hd_s, NCH * n + c)
                            nc.vector.scalar_tensor_tensor(out=m["s"][:, c % 8, :], in0=m["s"][:, (c - 1) % 8, :], scalar=dc[:, c:c + 1],
                                                           in1=u, op0=ALU.mult, op1=ALU.add).then_inc(hd_s, 1)
                    for c in range(NCH):
                        new_state(c)
                        if l == 0 and c < 8:
                            t, h2 = (2, h) if c < 4 else (0, h + 1)
                            if h2 < H:
                                values_low(h2, t, (2 * (c % 4), 2 * (c % 4) + 1))
                        elif l == 0 and h + 1 < H:
                            values_low(h + 1, 1, (c % 8,))
                        elif l == 1 and 4 <= c < 8:
                            values_low(h, 2, (2 * c - 8, 2 * c - 7))
                        elif l == 1 and c >= 8 and h + 1 < H:
                            values_low(h + 1, 0, (c % 8,))
                    if h + 1 < H and l == 1:
                        values_low(h + 1, 1)
                    dve.wait_ge(hd_dec, n + 1)
                    for f in range(SAMPLES // CPB):
                        dve.wait_ge(hd_su, fills(l, h, True) + f + 1)
                        states = m["s0"][:, f * CPB:(f + 1) * CPB, :]
                        nc.vector.tensor_tensor(states, states, ps[:, 2 + f, :].rearrange("p (b v) -> p b v", v=V), ALU.add).then_inc(hd_ss, CPB)
                    if h + 1 < H:
                        scores_keys(h + 1)
                    dve.wait_ge(hd_ms, n + 1)
                    link(nc.vector.tensor_tensor(m["sq"][:], ps[:, 6:6 + VB, 0:NT], m["g"][:, h * VB:(h + 1) * VB, :], ALU.mult))
                    if h == H - 1:
                        split(splits[0], groups)
                        splits[0] += 1
                    dve.wait_ge(hd_r, n + 1)
                    rb = m["rn"][:].unsqueeze(1).to_broadcast([P, VB, NT])
                    nc.vector.tensor_tensor(m["sq"][:], m["sq"][:], rb, ALU.mult).then_inc(hd_y, 1)
                db = first_block(l) + IN_BLOCKS[l]
                add_block(db, groups, 0)
                add_block(db + 1, groups, 1)
                layer_norm(3 * l)
                transposed(2 + 3 * l, TILES)
                split_ahead(db + 1, groups)
                t_ = st_att
                for c in range(2):
                    d2 = db + 2 + c
                    split_ahead(d2, groups)
                    dve.wait_ge(at_qs, 2 * l + c + 1)
                    b4 = 4 * (d2 % 2)
                    for b in range(4):
                        ins = nc.vector.tensor_tensor(t_["qs_lo"][:, 4 * c:4 * c + 4, :, b, 8 * b:8 * b + 8],
                                                      ps[:, b4:b4 + 4, PROMPT:NT].rearrange("p c (r b i) -> p c r b i", r=2, b=4)[:, :, :, b, :],
                                                      t_["qs_hi"][:, 4 * c:4 * c + 4, :, b, 8 * b:8 * b + 8].bitcast(F32), ALU.subtract)
                    ins.then_inc(evac[d2 % 2], 1)

                def keys_out(n):
                    for s in ((1, 3) if n == 0 else range(4)):
                        src = ps[:, s % 2, :].rearrange("p (b m) -> p b m", b=2)
                        if n == 0:
                            dve.wait_ge(at_tr, 4 * BATCHES * l + s + 1)
                            nc.vector.tensor_copy(kt0[:, 2 * s:2 * s + 2, :], src).then_inc(at_kv, 1)
                        else:
                            dve.wait_ge(at_ka, key_copies(l, n, s))
                            nc.vector.tensor_tensor(t_["kt_lo"][:, n % 2, 2 * s:2 * s + 2, :], src,
                                                    t_["kt_hi"][:, n % 2, 2 * s:2 * s + 2, :].bitcast(F32), ALU.subtract).then_inc(at_kv, 1)

                def row_max(t, banks, scored):
                    dve.wait_ge(at_sc, BATCHES * l + scored)
                    rows = P if t < 2 else 32
                    s = ps[0:rows, banks:banks + 2, :].rearrange("p a (b m) -> p (a b) m", b=2)
                    link(nc.vector.tensor_reduce(t_["rs"][0:rows, t, :], s, AX_X, ALU.max))
                    nc.vector.tensor_scalar(t_["mx"][0:rows, t, :], t_["rs"][0:rows, t, :], -float(D // XH) ** -0.5, None, ALU.mult).then_inc(at_max, 1)

                def normalise(t):
                    dve.wait_ge(at_exp, 4 * l + t + 1)
                    rows = P if t < 2 else 32
                    link(nc.vector.reciprocal(t_["rs"][0:rows, t, :], t_["sum"][0:rows, t, :]))
                    pp = t_["p"][0:rows, t]
                    nc.vector.tensor_tensor(pp, pp, t_["rs"][0:rows, t, :].unsqueeze(2).to_broadcast([rows, XH, MEM]), ALU.mult).then_inc(at_p, 1)

                keys_out(0)
                keys_out(1)
                row_max(0, 4, 1)
                row_max(1, 6, 1)
                keys_out(2)
                normalise(0)
                keys_out(3)
                normalise(1)
                keys_out(4)
                keys_out(5)
                row_max(2, 2, 5)
                keys_out(6)
                keys_out(7)
                normalise(2)
                keys_out(8)
                row_max(3, 4, 9)
                for r in range(2):
                    for mh in range(2):
                        dve.wait_ge(at_pth, 4 * l + 2 * r + mh + 1)
                        nc.vector.tensor_tensor(pts_lo[:, r, mh], ps[:, 6 - 2 * r + mh, :].rearrange("p (h s) -> p h s", h=XH),
                                                pts_hi[:, r, mh].bitcast(F32), ALU.subtract).then_inc(at_pte, 1)
                    if r == 0:
                        normalise(3)
                        for c in range(2):
                            dve.wait_ge(at_oh, 4 * l + c + 1)
                            nc.vector.tensor_tensor(xt_lo[:, 4 * c:4 * c + 4, 0:PROMPT], ps[:, 2 - 2 * c:4 - 2 * c, :].rearrange("p a (b q) -> p (a b) q", b=2),
                                                    xt_hi[:, 4 * c:4 * c + 4, 0:PROMPT].bitcast(F32), ALU.subtract).then_inc(at_ol, 1)
                        nc.vector.engine_nop().then_inc(w_low, BATCHES + 1)
                        nc.vector.engine_nop().then_inc(w_high, BATCHES + 1)
                        splits[0] = keys_no(l) + BATCHES + 1
                        split(splits[0], groups)
                        splits[0] += 1

                def rows_back(r):
                    dve.wait_ge(at_oh, 4 * l + 2 + r + 1)
                    cols = slice(PROMPT + 32 * r, PROMPT + 32 * r + 32)
                    nc.vector.tensor_tensor(xt_lo[:, :, cols], ps[:, 2 - 2 * r, 0:256].rearrange("p (k s) -> p k s", k=8),
                                            xt_hi[:, :, cols].bitcast(F32), ALU.subtract).then_inc(at_ol, 1)

                for _ in range(7):
                    split(splits[0], groups)
                    splits[0] += 1
                rows_back(0)
                for _ in range(2):
                    split(splits[0], groups)
                    splits[0] += 1
                rows_back(1)
                add_block(db + 4, groups, 0)
                add_block(db + 5, groups, 1)
                layer_norm(3 * l + 1)
                transposed(3 + 3 * l, TILES)
                m, s = st_moe, mo[l]
                dve.wait_ge(rt_e, l + 1)
                inverse(m["sc"][:])
                V_ = nc.vector
                link(V_.tensor_tensor(m["sel"][:], m["sc"][:], r_bias[:].unsqueeze(1).to_broadcast([P, TILES, EXPERTS]), ALU.add))
                for t in range(TILES):
                    sel = m["sel"][:, t, :].rearrange("p (g e) -> p g e", g=GROUPS)
                    V_.tensor_tensor(m["pair"][:, t, :, 0:3], sel[:, :, 0:3], sel[:, :, 1:4], ALU.add)
                    V_.tensor_tensor(m["pair"][:, t, :, 3:5], sel[:, :, 0:2], sel[:, :, 2:4], ALU.add)
                    ins = V_.tensor_tensor(m["pair"][:, t, :, 5:6], sel[:, :, 0:1], sel[:, :, 3:4], ALU.add)
                link(ins)
                link(V_.tensor_reduce(m["gs"][:], m["pair"][:], AX_X, ALU.max))
                link(V_.tensor_reduce(m["gm"][:], m["gs"][:], AX_X, ALU.max))

                def first_of(out, values, best, rank, n):
                    link(V_.tensor_tensor(out, values, best.unsqueeze(2).to_broadcast([P, TILES, n]), ALU.is_equal))
                    link(V_.tensor_tensor(out, out, rank.unsqueeze(1).to_broadcast([P, TILES, n]), ALU.mult))
                    link(V_.tensor_reduce(m["m1"][:], out, AX_X, ALU.max))
                    link(V_.tensor_tensor(out, out, m["m1"][:].unsqueeze(2).to_broadcast([P, TILES, n]), ALU.is_equal))

                first_of(m["g"][:], m["gs"][:], m["gm"][:], e_rank[:, 0:GROUPS], GROUPS)
                link(V_.memset(m["g"][64:P, 2, :], 0.0))
                V_.engine_nop().then_inc(rt_g, 1)
                for t in range(TILES):
                    ins = V_.tensor_copy(m["r1"][:, t, :].rearrange("p (g e) -> p g e", g=GROUPS), m["g"][:, t, :].unsqueeze(2).to_broadcast([P, GROUPS, EPG]))
                link(ins)
                link(V_.tensor_tensor(m["sel"][:], m["sel"][:], m["r1"][:], ALU.mult))
                link(V_.tensor_scalar(m["r1"][:], m["r1"][:], BIG, -BIG, ALU.mult, ALU.add))
                link(V_.tensor_tensor(m["sel"][:], m["sel"][:], m["r1"][:], ALU.add))
                link(V_.tensor_reduce(m["gm"][:], m["sel"][:], AX_X, ALU.max))
                first_of(m["r2"][:], m["sel"][:], m["gm"][:], e_rank[:], EXPERTS)
                link(V_.tensor_scalar(m["r1"][:], m["r2"][:], -2 * BIG, None, ALU.mult))
                link(V_.tensor_tensor(m["sel"][:], m["sel"][:], m["r1"][:], ALU.add))
                link(V_.tensor_reduce(m["gm"][:], m["sel"][:], AX_X, ALU.max))
                first_of(m["r3"][:], m["sel"][:], m["gm"][:], e_rank[:], EXPERTS)
                link(V_.tensor_tensor(m["r2"][:], m["r2"][:], m["r3"][:], ALU.add))
                link(V_.tensor_tensor(m["r2"][:], m["r2"][:], m["sc"][:], ALU.mult))
                link(V_.tensor_reduce(m["gm"][:], m["r2"][:], AX_X, ALU.add))
                link(V_.reciprocal(m["gm"][:], m["gm"][:]))
                link(V_.tensor_tensor(m["r2"][:], m["r2"][:], m["gm"][:].unsqueeze(2).to_broadcast([P, TILES, EXPERTS]), ALU.mult))
                for t in range(TILES):
                    ins = V_.tensor_reduce(comb4[:, t, :], m["r2"][:, t, :].rearrange("p (g e) -> p e g", g=GROUPS), AX_X, ALU.add)
                link(ins)
                dve.wait_ge(rt_pos, l + 1)
                link(V_.tensor_copy(m["pos"][:].rearrange("p t g -> p (t g)"), ps[:, 5, 0:TILES * GROUPS]))
                link(V_.tensor_scalar(m["p2"][:], m["pos"][:], 128.0, 384.0, ALU.is_ge, ALU.mult))
                link(V_.tensor_tensor(m["p2"][:], m["pos"][:], m["p2"][:], ALU.add))
                link(V_.tensor_scalar(m["pos"][:], m["pos"][:], 256.0, 384.0, ALU.is_ge, ALU.mult))
                link(V_.tensor_tensor(m["p2"][:], m["p2"][:], m["pos"][:], ALU.add))
                link(V_.tensor_tensor(m["p2"][:], m["p2"][:], g_base[:].unsqueeze(1).to_broadcast([P, TILES, GROUPS]), ALU.add))
                link(V_.tensor_tensor(m["p2"][:], m["p2"][:], m["g"][:], ALU.mult))
                link(V_.tensor_reduce(u_slot[:], m["p2"][:], AX_X, ALU.add))
                link(V_.tensor_scalar(u_slot[:], u_slot[:], -1.0, None, ALU.add))
                for t in range(TILES):
                    ins = V_.tensor_scalar(m["pick"][:, t, :], slot_no[:], u_slot[:, t:t + 1], None, ALU.is_equal)
                ins.then_inc(s["p"], 1)
                link(V_.tensor_reduce(m["mc"][:], ps[:, 5, TILES * GROUPS:TILES * GROUPS + GROUPS], AX_X, ALU.max))
                link(V_.tensor_scalar(m["mc2"][:], m["mc"][:], 128.0, 4.0, ALU.is_gt, ALU.mult))
                link(V_.tensor_scalar(m["mc"][:], m["mc"][:], 256.0, 4.0, ALU.is_gt, ALU.mult))
                link(V_.tensor_tensor(m["mc"][:], m["mc"][:], m["mc2"][:], ALU.add))
                link(V_.tensor_scalar(m["mc"][:], m["mc"][:], float(GROUPS - 1), None, ALU.add))
                V_.tensor_copy(n_last[:], m["mc"][0:1, :]).then_inc(rt_n, 1)
                V_.engine_nop().then_inc(s["h"], 1)
                V_.engine_nop().then_inc(s["side"], SKIPPED)
                V_.engine_nop().then_inc(s["read"], SKIPPED)
                dve.wait_ge(s["p"], 1)
                link(V_.tensor_scalar(u_slot[:], u_slot[:], -float(P), None, ALU.add))
                base = CHUNKS0 if l == 0 else CHUNKS1
                g0 = 0 if groups is None else groups
                def side(i, what, n, k, bank_no=7):
                    bank = ps[:, bank_no, :]
                    if what == "s":
                        dve.wait_ge(s["side"], k)
                        cols = x[:, n // 2, (n % 2) * NB:(n % 2 + 1) * NB]
                        V_.tensor_tensor(cols, cols, bank, ALU.add).then_inc(s["read"], 1)
                    elif what == "pt":
                        dve.wait_ge(s["side"], k)
                        if not isinstance(i, int):
                            dve.wait_ge(s["step"], i)
                        for t in range(TILES):
                            ins = V_.tensor_scalar(m["pick"][:, t, :], slot_no[:], u_slot[:, t:t + 1], None, ALU.is_equal)
                        ins.then_inc(s["p"], 1)
                        dve.wait_ge(s["p"], i + 2)
                        V_.tensor_scalar(u_slot[:], u_slot[:], -float(P), None, ALU.add).then_inc(s["step"], 1)
                    elif what == "t":
                        dve.wait_ge(s["xgh"], 2 * i + n + 3)
                        V_.tensor_tensor(xt_lo[:, 4 * n:4 * n + 4, 0:P], bank.rearrange("p (k s) -> p k s", k=4),
                                         xt_hi[:, 4 * n:4 * n + 4, 0:P].bitcast(F32), ALU.subtract).then_inc(s["read"], 1)

                def sums_out(i):
                    dve.wait_ge(s["yh"], i)
                    V_.tensor_tensor(m["y_lo"][:].rearrange("p (a c) -> p a c", a=2), ps[:, 4:6, :],
                                     m["y_hi"][:].rearrange("p (a c) -> p a c", a=2).bitcast(F32), ALU.subtract).then_inc(s["yl"], 1)

                def visit(i, first, last_one):
                    g = i if groups is None else groups + i
                    if not first:
                        sums_out(i)
                    uses = side_order(first, last_one)
                    for j in range(GCH):
                        for e in range(EPG):
                            if j == GU_LAST[e]:
                                dve.wait_ge(s["sil"], i * EPG + e + 1)
                                V_.scalar_tensor_tensor(out=m["h"][:, e % 2, :], in0=m["sil"][:], scalar=m["cw"][:, e:e + 1],
                                                        in1=ps[:, 2 * (e % 2) + 1, :], op0=ALU.mult, op1=ALU.mult).then_inc(s["h"], 1)
                        if j in T_AFTER:
                            e = T_AFTER[j]
                            dve.wait_ge(s["hth"], i * EPG + e + 1)
                            V_.tensor_tensor(m["ht_lo"][:, e % 2], ps[:, 6, :].rearrange("p (k s) -> p k s", k=4),
                                             m["ht_hi"][:, e % 2].bitcast(F32), ALU.subtract).then_inc(s["htl"], 1)
                        for k, (jj, what, n) in enumerate(uses):
                            if max(jj, 0) == j and not (what == "pt" and last_one):
                                side(i, what, n, side_start(i) + k + 1)
                        if j + MRING < GCH or not last_one:
                            split(base + j + MRING, g, (j + MRING) % MRING)

                for j in range(2):
                    split(base + j, g0, j % MRING)
                for n in range(2):
                    side(-1, "t", n, SKIPPED + 3 + n)
                for j in range(2, MRING):
                    split(base + j, g0, j % MRING)
                visit(0, True, False)
                dve.wait_ge(s["scaled"], 1)
                dve.wait_ge(rt_n, l + 1)
                nl = dve.value_load(n_last[0:1, 0:1], min_val=3, max_val=11)
                with dve.Fori(1, nl) as i:
                    visit(i, False, False)
                visit(nl, False, True)
                groups = nl + 1 if groups is None else groups + nl + 1
                sums_out(nl + 1)
                for n in range(6):
                    side(0, "s", n, nl * 12 + 13 + n, (7, 6, 0, 1, 2, 3)[n])
                    if n == 4:
                        dve.wait_ge(s["read"], nl * 12 + 13 + n)
                        half_stats(0)
                dve.wait_ge(s["read"], nl * 12 + 18)
                half_stats(1)
                layer_norm(3 * l + 2)
                if l == 0:
                    transposed(4, TILES)
                    dve.wait_ge(w_low, at(CHUNKS0 + 1, groups, GCH))
                    split(CHUNKS0 + 1, groups)
                    split(CHUNKS0 + 2, groups)
                    splits[0] += RING

        @block.tensor
        def _(pe):
            mm = nc.tensor.matmul

            def three(out, hi_w, lo_w, hi_x, lo_x, start, stop, x_moves, shared=False):
                for n, (w, v) in enumerate(((hi_w, hi_x), (hi_w, lo_x), (lo_w, hi_x)) if x_moves else
                                           ((hi_w, hi_x), (lo_w, hi_x), (hi_w, lo_x))):
                    lhs, rhs = (w, v) if x_moves else (v, w)
                    ins = mm(out, lhs, rhs, start=start and n == 0, stop=stop and n == 2, skip_group_check=shared)
                return ins

            def dense(db, groups, mode, tiles=TILES):
                par = db % 2
                if db >= 2:
                    pe.wait_ge(evac[par], db // 2)
                for half in range(2):
                    k = chunk_no(db) + half
                    r = slot_of(k)
                    pe.wait_ge(w_low, at(k + 1, groups, GCH))
                    for kc in range(4):
                        kt = 4 * half + kc
                        start, stop = kt == 0, kt == KT - 1
                        if mode == "T":
                            for n in range(4):
                                cols = slice(n * P, (n + 1) * P)
                                ins = three(ps[:, 4 * par + n, 0:NT], w_hi[:, r, kc, cols], w_lo[:, r, kc, cols],
                                            xt_hi[:, kt, 0:NT], xt_lo[:, kt, 0:NT], start, stop, True)
                        else:
                            for t in range(tiles):
                                toks = slice(t * P, (t + 1) * P)
                                ins = three(ps[:, 4 * par + t, :], w_hi[:, r, kc, :], w_lo[:, r, kc, :],
                                            xt_hi[:, kt, toks], xt_lo[:, kt, toks], start, stop, False)
                    ins.then_inc(w_used, 1)

            def transpose_in(u, src, tiles):
                for kt in range(KT):
                    if kt >= 4:
                        pe.wait_ge(xt_l, 8 * u + kt - 3)
                    for t in range(tiles):
                        ins = nc.tensor.transpose(ps[:, kt % 4, t * P:(t + 1) * P], src[:, t, kt * P:(kt + 1) * P], ident[:])
                    ins.then_inc(xt_ps, 1)
                pe.wait_ge(xt_l, 8 * u + 8)

            def head_scores(l, h):
                m, n = st_mix[l], l * 8 + h
                e = m["e"][:, h % 2]
                pe.wait_ge(hd_m, n + 1)
                if h:
                    pe.wait_ge(hd_msk, n)
                    pe.wait_ge(hd_kl, n)
                for t in range(TILES):
                    w = P if t < 2 else 64
                    toks = slice(t * P, t * P + w)
                    ins = mm(ps[0:w, 0, t * P:t * P + w], e[:, 1, toks], e[:, 0, toks], start=True, stop=True)
                ins.then_inc(hd_sc, 1)
                for t in range(TILES):
                    w = P if t < 2 else 64
                    ins = nc.tensor.transpose(ps[0:w, 1, t * P:(t + 1) * P], e[:, 3, t * P:t * P + w], ident[:])
                ins.then_inc(hd_tr, 1)

            def head(l, h):
                H, V, VB, _ = mixer_shape(l)
                m, n = st_mix[l], l * 8 + h
                e = m["e"][:, h % 2]
                vcols = slice(h * V, (h + 1) * V)

                def updates(f):
                    t, off = f * NB // (8 * V), f * NB % (8 * V)
                    if f >= 4:
                        pe.wait_ge(hd_s, NCH * n + (f - 3) * NB // V)
                    if off == 0:
                        pe.wait_ge(hd_vl, TILES * n + t + 1)
                    three(ps[:, 2 + f % 4, :], masked_values("hi", l, h, t)[:, off:off + NB], masked_values("lo", l, h, t)[:, off:off + NB],
                          m["kn_hi"][:, t, :], m["kn_lo"][:, t, :], True, True, False).then_inc(hd_u, 1)

                def read_state(c):
                    pe.wait_ge(hd_s, NCH * n + c)
                    for vb in range(VB):
                        ins = mm(ps[:, 6 + vb, c * CH:(c + 1) * CH], m["s"][:, (c - 1) % 8, vb * P:(vb + 1) * P],
                                 e[:, 2, c * CH:(c + 1) * CH], start=False, stop=True, skip_group_check=True)
                    ins.then_inc(hd_i, 1)

                pe.wait_ge(hd_kl, n + 1)
                if h:
                    pe.wait_ge(hd_ss, SAMPLES * n)
                for f in range(4):
                    if f == 3 and h:
                        pe.wait_ge(hd_ln, n)
                    updates(f)
                pe.wait_ge(hd_msk, n + 1)
                if h:
                    pe.wait_ge(hd_y, n)
                for vb in range(VB):
                    vc = slice(h * V + vb * P, h * V + (vb + 1) * P)
                    for t in range(TILES):
                        w = P if t < 2 else 64
                        mm(ps[:, 6 + vb, t * P:t * P + w], m["v"][0:w, t, vc], m["sc"][0:w, t, 0:w],
                           start=t == 0, stop=True, skip_group_check=True)
                pe.wait_ge(s0_in, 16 * (n + 1))
                for bb in range(SAMPLES):
                    toks = slice(PROMPT + 8 * bb, PROMPT + 8 * bb + 8)
                    for vb in range(VB):
                        mm(ps[:, 6 + vb, toks], m["s0"][:, bb, vb * P:(vb + 1) * P], e[:, 2, toks],
                           start=False, stop=True, skip_group_check=True)
                for c in range(1, NCH):
                    read_state(c)
                    if c % 2 == 0 and l == 1 and c // 2 + 3 < 8:
                        updates(c // 2 + 3)
                pe.wait_ge(hd_s, NCH * (n + 1))
                pe.wait_ge(hd_vl, TILES * n + 3)
                for f in range(SAMPLES * V // NB):
                    cols = slice(f * NB, (f + 1) * NB)
                    three(ps[:, 2 + f, :], masked_values("hi", l, h, 2)[0:64, cols], masked_values("lo", l, h, 2)[0:64, cols],
                          m["kn_hi"][0:64, 2, :], m["kn_lo"][0:64, 2, :], True, True, False).then_inc(hd_su, 1)

            def head_mean(l, h):
                H, V, VB, _ = mixer_shape(l)
                m, n = st_mix[l], l * 8 + h
                pe.wait_ge(hd_sq, n + 1)
                pe.wait_ge(hd_ss, SAMPLES * (n + 1))
                for vb in range(VB):
                    ins = mm(ps[:, 5, 0:NT], ones[:], m["sq"][:, vb, :], start=vb == 0, stop=vb == VB - 1)
                ins.then_inc(hd_ms, 1)

            pe.wait_ge(ident_made, 1)
            pe.wait_ge(mem_in, 16)
            transpose_in(0, st_kv["mem"], 2)
            for db in range(KV_BLOCKS):
                dense(db, None, "N", 2)
            pe.wait_ge(consts, 1)
            pe.wait_ge(consts_in, 160)
            pe.wait_ge(x_in, 32)
            pe.wait_ge(x_pad, 1)
            for par in range(2):
                pe.wait_ge(evac[par], KV_BLOCKS // 2)
            transpose_in(1, x, TILES)
            groups = None
            for l in range(LAYERS):
                H, V, VB, _ = mixer_shape(l)
                for nb in range(IN_BLOCKS[l]):
                    kind, c = block_kind(l, nb)
                    dense(first_block(l) + nb, groups, "N" if kind == "v" else "T")
                    if l == 1 and kind == "k":
                        pe.wait_ge(evac[0], (first_block(l) + nb - 1) // 2 + 1)
                        for kt in range(KT):
                            for r, xx in enumerate((xt_hi, xt_lo)):
                                ins = mm(ps[0:16, 3, 0:NT], w_lr[:, kt, :], xx[:, kt, 0:NT].bitcast(F32),
                                         start=kt == 0 and r == 0, stop=kt == KT - 1 and r == 1)
                        ins.then_inc(mx_lr, 1)
                        pe.wait_ge(mx_lrc, 1)
                        for hh in range(4):
                            if hh >= 2:
                                pe.wait_ge(mx_inv, 4 + hh - 1)
                            mm(ps[:, hh % 2, 0:NT], w_gk[:, hh * P:(hh + 1) * P], lr_t[:], start=True, stop=True).then_inc(mx_z, 1)
                        pe.wait_ge(mx_inv, 4 + 4)
                last = first_block(l) + IN_BLOCKS[l]
                for d in (last - 2, last - 1):
                    pe.wait_ge(evac[d % 2], d // 2 + 1)
                head_scores(l, 0)
                for h in range(H):
                    head(l, h)
                    if h + 1 < H:
                        head_scores(l, h + 1)
                    head_mean(l, h)
                pe.wait_ge(hd_fin, l * 8 + H)
                db = last
                dense(db, groups, "N")
                dense(db + 1, groups, "N")
                pe.wait_ge(ln_done, TILES * (3 * l + 1))
                transpose_in(2 + 3 * l, x, TILES)
                dense(db + 2, groups, "T")
                dense(db + 3, groups, "T")
                for d in (db + 2, db + 3):
                    pe.wait_ge(evac[d % 2], d // 2 + 1)
                t_ = st_att

                def keys_in(n):
                    k = keys_no(l) + n
                    pe.wait_ge(loaded[slot_of(k)], at(16 * loads_of(k), groups, 16 * GCH // MRING))
                    rows = raw[:, slot_of(k)].rearrange("p (t u) c -> p t (u c)", u=2)
                    for s in range(4):
                        if s >= 2 or n:
                            prev = (n, s - 2) if s >= 2 else (n - 1, s + 2)
                            pe.wait_ge(at_ka if prev[0] == 0 and s % 2 == 0 else at_kv, key_copies(l, *prev))
                        for b2 in range(2):
                            for mh in range(2):
                                ins = nc.tensor.transpose(ps[:, s % 2, b2 * MEM + mh * P:b2 * MEM + (mh + 1) * P],
                                                          rows[:, mh, (2 * s + b2) * P:(2 * s + b2 + 1) * P], ident[:])
                        ins.then_inc(at_tr, 1)

                def scores(n):
                    if n == 0:
                        pe.wait_ge(at_ka, key_copies(l, 0, 2))
                    pe.wait_ge(at_kv, key_copies(l, n, 3))
                    if n == 0:
                        for t in range(2):
                            for hh in range(XH):
                                for kc in range(2):
                                    ins = mm(ps[:, 4 + 2 * t + hh // 2, (hh % 2) * MEM:(hh % 2 + 1) * MEM], t_["q"][:, 2 * hh + kc, t * P:(t + 1) * P],
                                             kt0[:, 2 * hh + kc, :], start=kc == 0, stop=kc == 1)
                    else:
                        b = (n - 1) % 4
                        if n == 5:
                            pe.wait_ge(at_exp, 4 * l + 1)
                        for hh in range(XH):
                            out = ps[0:32, (2 if n < 5 else 4) + hh // 2, (hh % 2) * MEM:(hh % 2 + 1) * MEM]
                            for kc in range(2):
                                c = 2 * hh + kc
                                ins = three(out, t_["kt_hi"][:, n % 2, c, :], t_["kt_lo"][:, n % 2, c, :], t_["qs_hi"][:, c, (n - 1) // 4, b, :],
                                            t_["qs_lo"][:, c, (n - 1) // 4, b, :], b == 0 and hh % 2 == 0 and kc == 0, True, False, True)
                    ins.then_inc(at_sc, 1)

                keys_in(0)
                for n in range(1, BATCHES):
                    keys_in(n)
                    scores(n - 1)
                scores(BATCHES - 1)
                for r in range(4):
                    pe.wait_ge(at_p, 4 * l + r // 2 + 1)
                    if r < 2:
                        pe.wait_ge(at_kv, key_copies(l, BATCHES - 1, 3))
                    for hh in range(XH):
                        ins = nc.tensor.transpose(ps[:, (0, 1, 6, 7)[r], hh * P:(hh + 1) * P],
                                                  t_["p"][:, r // 2, hh, (r % 2) * P:(r % 2 + 1) * P], ident[:])
                    ins.then_inc(at_pt, 1)

                def samples_pt(r):
                    pe.wait_ge(at_p, 4 * l + 3 + r)
                    if r == 0:
                        pe.wait_ge(at_pte, 8 * l + 4)
                    for mh in range(2):
                        for hh in range(XH):
                            ins = mm(ps[:, 6 - 2 * r + mh, hh * P:(hh + 1) * P], t_["p"][0:32, 2 + r, hh, mh * P:(mh + 1) * P], batch_of[0:32, :],
                                     start=True, stop=True)
                        ins.then_inc(at_pt, 1)

                def samples_rows(r):
                    pe.wait_ge(at_on, 2 * l + r + 1)
                    pe.wait_ge(at_ol, 4 * l + r + 1)
                    for b8 in range(8):
                        ins = nc.tensor.transpose(ps[:, 2 - 2 * r, b8 * 32:(b8 + 1) * 32], o_rows[0:32, r, b8 * P:(b8 + 1) * P], ident[0:32, 0:32])
                    ins.then_inc(at_ot, 1)

                k = keys_no(l) + BATCHES
                pe.wait_ge(loaded[slot_of(k)], at(16 * loads_of(k), groups, 16 * GCH // MRING))
                rows = raw[:, slot_of(k)].rearrange("p (t u) c -> p t (u c)", u=2)
                pe.wait_ge(at_pte, 8 * l + 4)
                pe.wait_ge(at_exp, 4 * l + 3)
                samples_pt(0)
                for c in range(2):
                    for b4 in range(4):
                        for mh in range(2):
                            ins = mm(ps[:, 2 - 2 * c + b4 // 2, (b4 % 2) * PROMPT:(b4 % 2 + 1) * PROMPT], rows[:, mh, (4 * c + b4) * P:(4 * c + b4 + 1) * P],
                                     pt[:, mh, (4 * c + b4) // 2, :], start=mh == 0, stop=mh == 1)
                    if c == 0:
                        ins.then_inc(at_pv, 1)
                ins.then_inc(at_pv, 1)
                samples_pt(1)
                for n in range(1, BATCHES):
                    k, r, b = keys_no(l) + BATCHES + n, (n - 1) // 4, (n - 1) % 4
                    sl = slot_of(k)
                    if b == 0:
                        pe.wait_ge(at_pte, 8 * l + 4 + 2 * (r + 1))
                    pe.wait_ge(w_low, at(k + 1, groups, GCH))
                    for hh in range(XH):
                        out = ps[0:32, 6 - 2 * r + hh // 2, (hh % 2) * MEM:(hh % 2 + 1) * MEM]
                        for mh in range(2):
                            cols = slice((hh % 2) * MEM, (hh % 2 + 1) * MEM)
                            ins = three(out, w_hi[:, sl, 2 * mh + hh // 2, cols], w_lo[:, sl, 2 * mh + hh // 2, cols],
                                        pts_hi[:, r, mh, hh, 32 * b:32 * b + 32], pts_lo[:, r, mh, hh, 32 * b:32 * b + 32],
                                        b == 0 and hh % 2 == 0 and mh == 0, True, False, True)
                    ins.then_inc(w_used, BATCHES + 2 if n == 1 else 1)
                    if n == 5:
                        samples_rows(0)
                samples_rows(1)
                pe.wait_ge(at_ol, 4 * (l + 1))
                dense(db + 4, groups, "N")
                dense(db + 5, groups, "N")
                pe.wait_ge(ln_done, TILES * (3 * l + 2))
                transpose_in(3 + 3 * l, x, TILES)
                pe.wait_ge(rt_w, 2)
                for kt in range(KT):
                    ins = three(ps[0:EXPERTS, 4, 0:TILES * P], r_hi[:, kt, :], r_lo[:, kt, :], xt_hi[:, kt, :], xt_lo[:, kt, :],
                                kt == 0, kt == KT - 1, True)
                ins.then_inc(rt_ps, 1)
                m, s = st_moe, mo[l]
                pe.wait_ge(rt_c, l + 1)
                for t in range(TILES):
                    ins = nc.tensor.transpose(ps[:, 5, t * EXPERTS:(t + 1) * EXPERTS], m["rt"][:, t * P:(t + 1) * P], ident[0:EXPERTS, 0:EXPERTS])
                ins.then_inc(rt_ps, 1)
                m, s = st_moe, mo[l]
                pe.wait_ge(rt_g, l + 1)
                pe.wait_ge(rt_e, l + 1)
                for t in range(TILES):
                    for t2 in range(t + 1):
                        mm(ps[:, 5, t * GROUPS:(t + 1) * GROUPS], (before if t2 == t else ones)[:], m["g"][:, t2, :], start=t2 == 0, stop=t2 == t)
                for t in range(TILES):
                    ins = mm(ps[:, 5, TILES * GROUPS:(TILES + 1) * GROUPS], ones[:], m["g"][:, t, :], start=t == 0, stop=t == TILES - 1)
                ins.then_inc(rt_pos, 1)
                base = CHUNKS0 if l == 0 else CHUNKS1

                def side(i, what, n, k, bank_no=7):
                    if bank_no == 7:
                        pe.wait_ge(s["read"], k - 1)
                    if what == "cw":
                        for t in range(TILES):
                            ins = mm(ps[:, 7, 0:EPG], m["pick"][:, t, :].bitcast(F32), comb4[:, t, :], start=t == 0, stop=t == TILES - 1)
                    elif what == "s":
                        cols = slice((n % 2) * NB, (n % 2 + 1) * NB)
                        if n == 0:
                            pe.wait_ge(s["yl"], i)
                        mm(ps[:, bank_no, :], m["pick_t"][:, (n // 2) * P:(n // 2 + 1) * P], m["y_hi"][:, cols], start=True, stop=False)
                        ins = mm(ps[:, bank_no, :], m["pick_t"][:, (n // 2) * P:(n // 2 + 1) * P], m["y_lo"][:, cols], start=False, stop=True)
                    elif what == "pt":
                        for t in range(TILES):
                            ins = nc.tensor.transpose(ps[:, 7, t * P:(t + 1) * P], m["pick"][:, t, :].bitcast(F32), ident[:])
                    elif what == "g":
                        pe.wait_ge(s["p"], i + 2)
                        for t in range(TILES):
                            for r, xx in enumerate((m["xn_hi"], m["xn_lo"])):
                                ins = mm(ps[:, 7, :], m["pick"][:, t, :], xx[:, t, n * NB:(n + 1) * NB],
                                         start=t == 0 and r == 0, stop=t == TILES - 1 and r == 1)
                    else:
                        for kc in range(4):
                            c = 4 * n + kc
                            ins = nc.tensor.transpose(ps[:, 7, kc * P:(kc + 1) * P], m["xg"][:, c * P:(c + 1) * P], ident[:])
                    ins.then_inc(s["side"], 1)

                def visit(i, first, last_one):
                    g = i if groups is None else groups + i
                    uses = side_order(first, last_one)
                    side(i, "cw", 0, side_start(i) + 1)
                    for j, (what, e, half) in enumerate(MOE_ORDER):
                        _, hi, lo = parts(j % MRING)
                        if what == "gate" and half == 0 and not (first and e < 2):
                            pe.wait_ge(s["h"], i * EPG + e)
                        if what == "down" and half == 0:
                            pe.wait_ge(s["htl"], i * EPG + e + 1)
                            if e == 0 and first:
                                pe.wait_ge(rt_n, l + 1)
                            elif e == 0:
                                pe.wait_ge(s["yl"], i)
                        pe.wait_ge(w_low, at(base + j + 1, g, GCH))
                        for kc in range(4):
                            if what == "down":
                                ins = three(ps[:, 4 + half, :], hi[:, kc, :], lo[:, kc, :], m["ht_hi"][:, e % 2, kc, :],
                                            m["ht_lo"][:, e % 2, kc, :], e == 0 and kc == 0, e == EPG - 1 and kc == 3, False)
                            else:
                                kt = 4 * half + kc
                                ins = three(ps[:, 2 * (e % 2) + (what == "up"), :], hi[:, kc, :], lo[:, kc, :], xt_hi[:, kt, 0:P],
                                            xt_lo[:, kt, 0:P], kt == 0, kt == KT - 1, False)
                        ins.then_inc(w_used, 1)
                        if j in T_AFTER:
                            e2 = T_AFTER[j]
                            pe.wait_ge(s["h"], i * EPG + e2 + 2)
                            if e2 or not first:
                                pe.wait_ge(s["htl"], i * EPG + e2)
                            for kc in range(4):
                                ins = nc.tensor.transpose(ps[:, 6, kc * P:(kc + 1) * P], m["h"][:, e2 % 2, kc * P:(kc + 1) * P], ident[:])
                            ins.then_inc(s["t"], 1)
                        for k, (jj, what2, n2) in enumerate(uses):
                            if jj == j:
                                side(i, what2, n2, side_start(i) + k + 1)

                pe.wait_ge(s["xl"], 1)
                for k, (what, n) in enumerate((("g", 0), ("g", 1), ("t", 0), ("t", 1))):
                    side(-1, what, n, SKIPPED + k + 1)
                visit(0, True, False)
                pe.wait_ge(rt_n, l + 1)
                nl = pe.value_load(n_last[0:1, 0:1], min_val=3, max_val=11)
                with pe.Fori(1, nl) as i:
                    visit(i, False, False)
                visit(nl, False, True)
                for n in range(6):
                    side(nl + 1, "s", n, nl * 12 + 13 + n, (7, 6, 0, 1, 2, 3)[n])
                groups = nl + 1 if groups is None else groups + nl + 1
                if l == 0:
                    pe.wait_ge(ln_done, TILES * 3)
                    transpose_in(4, x, TILES)


_INS = ["x_prompt", "x_sample", "state_hgrn", "state_gla", "cache_mem_k", "cache_mem_v", "mem_prompt",
        "hgrn_w_in", "hgrn_lb_logits", "hgrn_norm_g", "hgrn_w_out", "gla_w_in", "gla_w_gk2", "gla_b_gk2",
        "gla_norm_g", "gla_w_out", "xattn_w_q", "xattn_w_kv", "xattn_w_o", "router_w", "router_bias",
        "moe_w_gate", "moe_w_up", "moe_w_down", "ln_g", "ln_b"]
_OUTS = [("y_prompt", (1, PROMPT, D)), ("y_sample", (SAMPLES, SAMPLE_T, D)),
         ("state_hgrn_prompt", (1, 1, 8, 128, 128)), ("state_gla_prompt", (1, 1, 4, 128, 256)),
         ("mem_k_prompt", (2, 1, MEM, XH, 256)), ("mem_v_prompt", (2, 1, MEM, XH, 256)),
         ("state_hgrn_sample", (1, 8, 8, 128, 128)), ("state_gla_sample", (1, 8, 4, 128, 256))]


def kernel(**inputs):
    import numpy as _np
    import concourse.bacc as _bacc
    from concourse.bass_utils import run_bass_kernel_spmd as _run

    nc = _bacc.Bacc("TRN2", target_bir_lowering=False, num_devices=1)
    arrays, aps = {}, {}
    for name in _INS:
        arrays[f"in_{name}"] = _np.ascontiguousarray(inputs[name])
        aps[name] = nc.dram_tensor(f"in_{name}", arrays[f"in_{name}"].shape, F32, kind="ExternalInput").ap()
    for name, shape in _OUTS:
        aps[name] = nc.dram_tensor(f"out_{name}", shape, F32, kind="ExternalOutput").ap()
    decoder_step(nc, aps)
    r = _run(nc, [arrays], core_ids=[0])
    return tuple(r.results[0][f"out_{name}"] for name, _ in _OUTS)
```
